# Optimizing a Trainium2 kernel written in Bass

```python
import math
import jax, jax.numpy as jnp
from jax import lax
import numpy as np

D_MODEL = 1024
BATCH = 1
SEQ = 256
DEPTH = 2

HEAD_DIM = 64
A_HEADS = 4
A_QK = 2 * HEAD_DIM
A_V = 2 * HEAD_DIM
A_W = A_HEADS * A_V
B_GROUPS = ((128, 1), (512, 4), (2048, 16))
B_HEADS = 6
B_QW = len(B_GROUPS) * B_HEADS * HEAD_DIM
B_W = B_HEADS * HEAD_DIM
C_HEADS = 6
C_W = C_HEADS * HEAD_DIM
N_BRANCH = 3
BLOCK = 128
N_BUCKETS = 32
REL_MAX_DIST = 2048
N_BIAS_HEADS = 2 * A_HEADS + len(B_GROUPS) * B_HEADS
D_FF = 2816
N_EXPERTS = 8
TOP_K = 2
D_FF_EXPERT = 3584
N_DENSE = (DEPTH + 1) // 2
N_MOE = DEPTH // 2
EPS = 1e-6
IN_SIZES = (A_HEADS * A_QK, A_HEADS * A_QK, A_W, B_QW, B_QW, B_QW, C_W, C_W, C_W, C_HEADS, N_BRANCH * D_MODEL)
N_IN = sum(IN_SIZES)

kernel_name = 'hybrid_diff_dilated_fox_moe_block'

def rms_norm(x, g):
    xf = x.astype(jnp.float32)
    y = xf * lax.rsqrt(jnp.mean(xf * xf, axis=-1, keepdims=True) + EPS)
    return (y * g.astype(jnp.float32)).astype(x.dtype)

def t5_bucket(dist):
    n = jnp.maximum(dist, 0)
    max_exact = N_BUCKETS // 2
    nf = jnp.maximum(n, 1).astype(jnp.float32)
    large = max_exact + (jnp.log(nf / max_exact) / math.log(REL_MAX_DIST / max_exact)
                         * (N_BUCKETS - max_exact)).astype(jnp.int32)
    large = jnp.minimum(large, N_BUCKETS - 1)
    return jnp.where(n < max_exact, n, large)

def diff_attention(q, k, v, lam, bias_tab):
    S = q.shape[1]
    H = q.shape[2]
    scale = HEAD_DIM ** -0.5
    outs = []
    for i in range(S // BLOCK):
        q0 = i * BLOCK
        L = q0 + BLOCK
        s = jnp.einsum('bqhmd,bkhmd->bhmqk', q[:, q0:L], k[:, :L]).astype(jnp.float32) * scale
        dist = (q0 + jnp.arange(BLOCK))[:, None] - jnp.arange(L)[None, :]
        bias = bias_tab[t5_bucket(dist)].reshape(BLOCK, L, H, 2).transpose(2, 3, 0, 1)
        s = jnp.where(dist >= 0, s + bias.astype(jnp.float32), -jnp.inf)
        p = jax.nn.softmax(s, axis=-1)
        w = p[:, :, 0] - lam * p[:, :, 1]
        outs.append(jnp.einsum('bhqk,bkhe->bqhe', w.astype(v.dtype), v[:, :L]))
    return jnp.concatenate(outs, axis=1)

def forgetting_attention(q, k, v, log_f):
    S = q.shape[1]
    scale = HEAD_DIM ** -0.5
    F = jnp.moveaxis(jnp.cumsum(log_f, axis=1), 1, 2)
    outs = []
    for i in range(S // BLOCK):
        q0 = i * BLOCK
        L = q0 + BLOCK
        s = jnp.einsum('bqhd,bkhd->bhqk', q[:, q0:L], k[:, :L]).astype(jnp.float32) * scale
        decay = F[:, :, q0:L, None] - F[:, :, None, :L]
        causal = (q0 + jnp.arange(BLOCK))[:, None] >= jnp.arange(L)[None, :]
        s = jnp.where(causal, s + decay, -jnp.inf)
        p = jax.nn.softmax(s, axis=-1)
        outs.append(jnp.einsum('bhqk,bkhd->bqhd', p.astype(v.dtype), v[:, :L]))
    return jnp.concatenate(outs, axis=1)

def dilated_attention(q, k, v, bias_tab):
    B_, S = q.shape[0], q.shape[1]
    scale = HEAD_DIM ** -0.5
    outs, lses = [], []
    for g, (window, dil) in enumerate(B_GROUPS):
        n_back = window // dil
        M = S // dil
        nblk = -(-M // BLOCK)
        Mp = nblk * BLOCK

        def strided(t):
            return jnp.moveaxis(t.reshape(B_, M, dil, B_HEADS, HEAD_DIM), 2, 1)

        def blk(t):
            return t.reshape(B_, dil, nblk, BLOCK, B_HEADS, HEAD_DIM)

        qg, kg, vg = strided(q[:, :, g]), strided(k[:, :, g]), strided(v[:, :, g])
        qblk = blk(jnp.pad(qg, ((0, 0), (0, 0), (0, Mp - M), (0, 0), (0, 0))))
        kp = jnp.pad(kg, ((0, 0), (0, 0), (BLOCK, Mp - M), (0, 0), (0, 0)))
        vp = jnp.pad(vg, ((0, 0), (0, 0), (BLOCK, Mp - M), (0, 0), (0, 0)))
        kblk = jnp.concatenate([blk(kp[:, :, :Mp]), blk(kp[:, :, BLOCK:])], axis=3)
        vblk = jnp.concatenate([blk(vp[:, :, :Mp]), blk(vp[:, :, BLOCK:])], axis=3)
        s = jnp.einsum('brnqhd,brnkhd->brnhqk', qblk, kblk).astype(jnp.float32) * scale
        qi = jnp.arange(BLOCK)[:, None]
        kj = jnp.arange(2 * BLOCK)[None, :]
        dm = qi + BLOCK - kj
        key_m = (jnp.arange(nblk)[:, None, None] - 1) * BLOCK + kj[None]
        valid = (dm >= 0) & (dm <= n_back) & (key_m >= 0)
        bias = bias_tab[:, g * B_HEADS:(g + 1) * B_HEADS][t5_bucket(dm * dil)]
        bias = jnp.moveaxis(bias, -1, 0).astype(jnp.float32)
        s = jnp.where(valid[None, None, :, None], s + bias, -jnp.inf)
        m = jnp.max(s, axis=-1, keepdims=True)
        e = jnp.exp(s - m)
        den = jnp.sum(e, axis=-1)
        o = jnp.einsum('brnhqk,brnkhd->brnqhd', e.astype(v.dtype), vblk).astype(jnp.float32)
        o = o / jnp.moveaxis(den, -1, -2)[..., None]
        lse = jnp.moveaxis(m[..., 0] + jnp.log(den), -1, -2)

        def unstrided(t):
            t = t.reshape(B_, dil, Mp, *t.shape[4:])[:, :, :M]
            return jnp.moveaxis(t, 1, 2).reshape(B_, S, *t.shape[3:])

        outs.append(unstrided(o))
        lses.append(unstrided(lse))
    alpha = jax.nn.softmax(jnp.stack(lses), axis=0)
    return jnp.sum(alpha[..., None] * jnp.stack(outs), axis=0)

def hybrid_mixer(h, w_in, b_f, lq1, lk1, lq2, lk2, subln_g, lam_init, rel_bias,
                 w_br_a, w_br_b, w_br_c, w_out):
    B_, S, _ = h.shape
    proj = h @ w_in
    offsets = np.cumsum(IN_SIZES)[:-1].tolist()
    qa, ka, va, qb, kb, vb, qc, kc, vc, f_logit, gate_logit = jnp.split(proj, offsets, axis=-1)
    lam = (jnp.exp(jnp.sum((lq1 * lk1).astype(jnp.float32)))
           - jnp.exp(jnp.sum((lq2 * lk2).astype(jnp.float32))) + lam_init)
    oa = diff_attention(qa.reshape(B_, S, A_HEADS, 2, HEAD_DIM), ka.reshape(B_, S, A_HEADS, 2, HEAD_DIM),
                        va.reshape(B_, S, A_HEADS, A_V), lam, rel_bias[:, :2 * A_HEADS])
    oa = (rms_norm(oa, subln_g) * (1.0 - lam_init)).reshape(B_, S, A_W)
    G = len(B_GROUPS)
    ob = dilated_attention(qb.reshape(B_, S, G, B_HEADS, HEAD_DIM), kb.reshape(B_, S, G, B_HEADS, HEAD_DIM),
                           vb.reshape(B_, S, G, B_HEADS, HEAD_DIM), rel_bias[:, 2 * A_HEADS:])
    ob = ob.astype(h.dtype).reshape(B_, S, B_W)
    log_f = jax.nn.log_sigmoid(f_logit.astype(jnp.float32) + b_f.astype(jnp.float32))
    oc = forgetting_attention(qc.reshape(B_, S, C_HEADS, HEAD_DIM), kc.reshape(B_, S, C_HEADS, HEAD_DIM),
                              vc.reshape(B_, S, C_HEADS, HEAD_DIM), log_f).reshape(B_, S, C_W)
    gates = jax.nn.sigmoid(gate_logit).reshape(B_, S, N_BRANCH, D_MODEL)
    merged = (gates[:, :, 0] * (oa @ w_br_a) + gates[:, :, 1] * (ob @ w_br_b)
              + gates[:, :, 2] * (oc @ w_br_c))
    return merged @ w_out

def swiglu(h, wg, wu, wd):
    return (jax.nn.silu(h @ wg) * (h @ wu)) @ wd

def moe_swiglu(h, w_router, wg, wu, wd):
    logits = (h @ w_router).astype(jnp.float32)
    top_val, top_idx = lax.top_k(logits, TOP_K)
    top_w = jax.nn.softmax(top_val, axis=-1)
    gate = jnp.sum(jax.nn.one_hot(top_idx, N_EXPERTS, dtype=jnp.float32) * top_w[..., None], axis=-2)
    out = jnp.zeros_like(h)
    for e in range(N_EXPERTS):
        out = out + gate[..., e:e + 1].astype(h.dtype) * swiglu(h, wg[e], wu[e], wd[e])
    return out

def setup_inputs(seed: int = 0) -> dict:
    key = jax.random.key(seed)
    ks = jax.random.split(key, 26)

    def nrm(k, shape, s):
        return jax.random.normal(k, shape, jnp.float32) * s

    D = D_MODEL
    return {
        'x': nrm(ks[0], (BATCH, SEQ, D), 1.0),
        'c': nrm(ks[1], (BATCH, D), 1.0),
        'norm_mix_g': 1.0 + nrm(ks[2], (DEPTH, D), 0.02),
        'norm_ffn_g': 1.0 + nrm(ks[3], (DEPTH, D), 0.02),
        'w_mod': nrm(ks[4], (DEPTH, D, 6 * D), 0.5 * D ** -0.5),
        'b_mod': nrm(ks[5], (DEPTH, 6 * D), 0.02),
        'w_in': nrm(ks[6], (DEPTH, D, N_IN), D ** -0.5),
        'b_forget': 2.0 + nrm(ks[7], (DEPTH, C_HEADS), 0.5),
        'lam_q1': nrm(ks[8], (DEPTH, HEAD_DIM), 0.1),
        'lam_k1': nrm(ks[9], (DEPTH, HEAD_DIM), 0.1),
        'lam_q2': nrm(ks[10], (DEPTH, HEAD_DIM), 0.1),
        'lam_k2': nrm(ks[11], (DEPTH, HEAD_DIM), 0.1),
        'subln_g': 1.0 + nrm(ks[12], (DEPTH, A_V), 0.02),
        'rel_bias': nrm(ks[13], (N_BUCKETS, N_BIAS_HEADS), 0.5),
        'w_br_a': nrm(ks[14], (DEPTH, A_W, D), A_W ** -0.5),
        'w_br_b': nrm(ks[15], (DEPTH, B_W, D), B_W ** -0.5),
        'w_br_c': nrm(ks[16], (DEPTH, C_W, D), C_W ** -0.5),
        'w_out': nrm(ks[17], (DEPTH, D, D), D ** -0.5),
        'w_ff_gate': nrm(ks[18], (N_DENSE, D, D_FF), D ** -0.5),
        'w_ff_up': nrm(ks[19], (N_DENSE, D, D_FF), D ** -0.5),
        'w_ff_down': nrm(ks[20], (N_DENSE, D_FF, D), D_FF ** -0.5),
        'w_router': nrm(ks[21], (N_MOE, D, N_EXPERTS), D ** -0.5),
        'w_exp_gate': nrm(ks[22], (N_MOE, N_EXPERTS, D, D_FF_EXPERT), D ** -0.5),
        'w_exp_up': nrm(ks[23], (N_MOE, N_EXPERTS, D, D_FF_EXPERT), D ** -0.5),
        'w_exp_down': nrm(ks[24], (N_MOE, N_EXPERTS, D_FF_EXPERT, D), D_FF_EXPERT ** -0.5),
        'final_norm_g': 1.0 + nrm(ks[25], (D,), 0.02),
    }

def reference(x, c, norm_mix_g, norm_ffn_g, w_mod, b_mod, w_in, b_forget, lam_q1, lam_k1, lam_q2,
              lam_k2, subln_g, rel_bias, w_br_a, w_br_b, w_br_c, w_out, w_ff_gate, w_ff_up, w_ff_down,
              w_router, w_exp_gate, w_exp_up, w_exp_down, final_norm_g):
    for l in range(DEPTH):
        lam_init = 0.8 - 0.6 * math.exp(-0.3 * l)
        mod = jax.nn.silu(c) @ w_mod[l] + b_mod[l]
        sh1, sc1, g1, sh2, sc2, g2 = jnp.split(mod[:, None, :], 6, axis=-1)
        h = rms_norm(x, norm_mix_g[l]) * (1.0 + sc1) + sh1
        x = x + g1 * hybrid_mixer(h, w_in[l], b_forget[l], lam_q1[l], lam_k1[l], lam_q2[l], lam_k2[l],
                                  subln_g[l], lam_init, rel_bias, w_br_a[l], w_br_b[l], w_br_c[l], w_out[l])
        h = rms_norm(x, norm_ffn_g[l]) * (1.0 + sc2) + sh2
        if l % 2 == 0:
            f = swiglu(h, w_ff_gate[l // 2], w_ff_up[l // 2], w_ff_down[l // 2])
        else:
            f = moe_swiglu(h, w_router[l // 2], w_exp_gate[l // 2], w_exp_up[l // 2], w_exp_down[l // 2])
        x = x + g2 * f
    return rms_norm(x, final_norm_g)


_drawn_inputs = setup_inputs


def setup_inputs(seed=0):
    import zlib

    import numpy as np

    out = dict(_drawn_inputs(seed))
    spreads = {}
    factors = {'norm_mix_g': 8.0,
     'norm_ffn_g': 3.878,
     'lam_q1': 5.398,
     'lam_k1': 4.885,
     'lam_q2': 4.981,
     'lam_k2': 5.284,
     'subln_g': 8.0,
     'final_norm_g': 2.809}
    for name, (base, spread) in spreads.items():
        noise = np.random.default_rng([zlib.crc32(name.encode()), seed]).standard_normal(out[name].shape)
        drawn = base * np.exp(spread * noise) if base else spread * noise
        out[name] = __import__('jax').numpy.asarray(drawn.astype(out[name].dtype))
    for name, factor in factors.items():
        out[name] = (out[name] * factor).astype(out[name].dtype)
    return out
```

```python
import math
from contextlib import ExitStack

import concourse.bass as bass
import numpy as np
from concourse import mybir

F32 = mybir.dt.float32
F32R = mybir.dt.float32r
I32 = mybir.dt.int32
U32 = mybir.dt.uint32
ALU = mybir.AluOpType
ACT = mybir.ActivationFunctionType
AX_X = mybir.AxisListType.X

P = 128
S = 256
NT = S // P
D = 1024
KB = D // P
DEPTH = 2
HD = 64
A_HEADS, B_HEADS, C_HEADS, GROUPS = 4, 6, 6, ((128, 1), (512, 4), (2048, 16))
G = len(GROUPS)
A_W, B_W, C_W = A_HEADS * 2 * HD, B_HEADS * HD, C_HEADS * HD
QA, KA, VA = 0, A_W, 2 * A_W
QB = 3 * A_W
KBC, VB = QB + G * B_W, QB + 2 * G * B_W
QC = QB + 3 * G * B_W
KC, VC = QC + C_W, QC + 2 * C_W
FC = QC + 3 * C_W
GC = FC + C_HEADS
N_IN = GC + 3 * D
N_BUCKETS, REL_MAX_DIST = 32, 2048
N_BIAS = 2 * A_HEADS + G * B_HEADS
D_FF = 2816
NE, FE = 8, 3584
EPS = 1e-6
VW = A_W + G * B_W + C_W
OW = (A_W + B_W + C_W) // P
BLOCKED = -1e30
NJ = 384
CH = 512
NC = FE // CH

UM = 1024
R, H = 6, 3
RE, HE = 12, 6


def lam_init(l):
    return 0.8 - 0.6 * math.exp(-0.3 * l)


def shape_tables():
    dist = S - 1 - np.arange(NJ)
    n = np.maximum(dist, 0)
    exact = N_BUCKETS // 2
    nf = np.maximum(n, 1).astype(np.float32)
    large = exact + (np.log(nf / np.float32(exact)) / np.float32(math.log(REL_MAX_DIST / exact))
                     * np.float32(N_BUCKETS - exact)).astype(np.int32)
    bucket = np.where(n < exact, n, np.minimum(large, N_BUCKETS - 1))
    onehot = (np.arange(N_BUCKETS)[:, None] == bucket[None]).astype(np.float32)
    sees = np.tile(dist >= 0, (N_BIAS + 1, 1))
    for g, (window, dil) in enumerate(GROUPS):
        r = slice(2 * A_HEADS + g * B_HEADS, 2 * A_HEADS + (g + 1) * B_HEADS)
        sees[r] &= ((dist % dil == 0) & (dist <= window))[None]
    return onehot, np.where(sees, 0.0, BLOCKED).astype(np.float32)


class Unit:

    def __init__(self, src, shape, mod=None):
        self.src, self.shape, self.mod = src, shape, mod


def mixer_ops(l, w):
    w_in = w["w_in"][l].rearrange("(kb p) n -> p kb n", p=P)
    w_br = [w[n][l].rearrange("(kb p) n -> p kb n", p=P) for n in ("w_br_a", "w_br_b", "w_br_c")]
    w_out = w["w_out"][l].rearrange("(kb p) n -> p kb n", p=P)

    def qk(pair):
        if pair < 4:
            cols = [QA + P * pair, KA + P * pair]
        elif pair < 7:
            cols = [base + g * B_W + P * (pair - 4) for base in (QB, KBC) for g in range(G)]
        else:
            cols = [QC + P * (pair - 7), KC + P * (pair - 7)]
        half = len(cols) // 2
        return [("qk", Unit(w_in[:, :, c:c + P], (KB, P)), dict(pair=pair, j=(j % half) + 3 * (j // half)))
                for j, c in enumerate(cols)]

    def wide(kind, view, kbs, c0, width, **args):
        ops = []
        for k0 in range(0, kbs, 2):
            nk = min(2, kbs - k0)
            ops.append((kind, Unit(view[:, k0:k0 + nk, c0:c0 + width], (nk, width)),
                        dict(k0=k0, first=k0 == 0, last=k0 + nk == kbs, width=width, **args)))
        return ops

    va = wide("v", w_in, KB, VA, A_W, dst=0)
    vb = [o for c in range(0, G * B_W, 512)
          for o in wide("v", w_in, KB, VB + c, min(512, G * B_W - c), dst=A_W + c)]
    vc = wide("v", w_in, KB, VC, C_W, dst=A_W + G * B_W)

    def merge(b, n):
        gate = wide("gate", w_in, KB, GC + b * D + n * 512, 512, b=b, n=n)
        lift = wide("lift", w_br[b], (4, 3, 3)[b], n * 512, 512, b=b, n=n)
        return gate + lift

    fills = {}
    order_a = [qk(1) + vb[:4], vb[4:8], qk(2) + vb[8:10], vb[10:], qk(3) + vc[:2], vc[2:], qk(4)[:3], qk(4)[3:]]
    for t in range(8):
        fills[t] = order_a[t]
    for i, p in enumerate((5, 6)):
        fills[8 + 2 * i], fills[9 + 2 * i] = qk(p)[:3], qk(p)[3:]
    fills[12], fills[13] = qk(7), merge(0, 0)
    fills[14], fills[15] = qk(8), merge(0, 1)
    fills[16], fills[17] = qk(9), merge(1, 0)
    fills[18], fills[19] = merge(1, 1), []
    ops = [("forget", None, {})] + qk(0) + [("cumsum", None, {})] + va
    for t in range(20):
        f = fills[t]
        cut = (len(f) + 1) // 2
        ops += [("scores", None, dict(t=t))]
        ops += f[:1] + [("weigh", None, dict(t=t))] + f[1:cut] + [("turn_probs", None, dict(t=t))] + f[cut:]
        if t:
            ops += [("turn_out", None, dict(t=t - 1))]
        ops += [("values", None, dict(t=t))]
    ops += [("turn_out", None, dict(t=19))]
    ops += merge(2, 0) + merge(2, 1)
    ops += [("turn_merged", None, {})]
    for n in range(2):
        ops += wide("out", w_out, KB, n * 512, 512, n=n)

    mods = [(l, 1), (l, 2)] + [(l + 1, 0)] * (l + 1 < DEPTH)
    todo = [o for (ml, part) in mods for o in mod_ops(ml, part, w)]
    woven, done = [("gain", None, dict(src="norm_ffn_g", l=l))], 0
    if l + 1 < DEPTH:
        todo.insert(len(todo) - 8, ("gain", None, dict(src="norm_mix_g", l=l + 1)))
    last = max(i for i, o in enumerate(ops) if o[0] == "turn_merged") - 8
    for i, o in enumerate(ops):
        woven.append(o)
        if i < last:
            upto = min(len(todo), len(todo) * (i + 1) // (last - 1))
            woven += todo[done:upto]
            done = upto
    assert done == len(todo)
    if l + 1 == DEPTH:
        woven.append(("gain", None, dict(src="final_norm_g", l=0)))
    return woven


def mod_ops(l, part, w):
    view = w["w_mod"][l].rearrange("(kb p) n -> p kb n", p=P)
    ops = []
    for kb in range(KB):
        for half in range(2):
            c0 = part * 2048 + half * UM
            ops.append(("mod", Unit(view[:, kb:kb + 1, c0:c0 + UM], (1, UM), mod=(l, part, kb, half)), {}))
    return ops + [("mod_sum", None, dict(l=l, part=part, n=n)) for n in range(4)]


class Plan:

    def __init__(self, w):
        self.raw_n = self.split_n = self.mod_n = 0
        self.owner = [None] * R
        self.segments = {}
        self.units = {}
        self.bank = [0, 0]
        self.turned = self.upper = 0
        self.sums = 0
        self.gain_used = None
        self.lifts = self.gates = 0
        self.qk_ready, self.v_ready = {}, {}
        self.qk_turn = 0
        self.misc = 1
        self.outs_ready = {}
        self.part_ready = {}
        self.tasks = self.scores = 0
        self.segment("start", [("gain", None, dict(src="norm_mix_g", l=0))] + mod_ops(0, 0, w))
        self.segment("mix0", mixer_ops(0, w))

    def unit(self, u):
        u.raw = self.raw_n % R
        u.landed = 16 * (self.raw_n // R + 1)
        u.waits = self.owner[u.raw]
        if u.mod is None:
            u.split = self.split_n
            u.hl = self.split_n % H
            self.split_n += 1
            self.owner[u.raw] = ("split", u.split)
        else:
            u.nth = self.mod_n
            self.mod_n += 1
            self.owner[u.raw] = ("mod", u.nth)
        self.raw_n += 1

    def segment(self, name, ops):
        out = []
        for kind, unit, a in ops:
            a = dict(a)
            if unit is not None:
                self.unit(unit)
            if kind == "qk":
                b = self.qk_turn % 2
                self.qk_turn += 1
                a.update(bank=b, uses=self.bank[b])
                self.bank[b] += 1
                self.qk_ready[a["pair"]] = tuple(self.bank)
            elif kind in ("v", "gate", "lift", "out"):
                a["uses"] = tuple(self.bank)
                if a["last"]:
                    self.bank = [self.bank[0] + 1, self.bank[1] + 1]
                    if kind == "v":
                        self.v_ready[sum(a["dst"] >= e for e in (A_W, A_W + G * B_W))] = tuple(self.bank)
                    if kind == "gate":
                        self.gates += 1
                        a["nth"] = self.gates
                    if kind == "lift":
                        self.lifts += 1
                        a["nth"] = self.lifts
            elif kind in ("turn_out", "cumsum", "mod_sum", "forget"):
                a["misc"] = self.misc
                self.misc += 1
                if kind == "mod_sum":
                    a["nth"] = self.sums
                    self.sums += 1
                    self.part_ready[a["l"], a["part"]] = self.misc
                    if not plain_part(a["part"], a["n"]):
                        self.gain_used = self.misc
            elif kind == "scores":
                pair = a["t"] // 2
                a.update(n=self.tasks, ready=self.qk_ready[pair], turned=self.turned, upper=self.upper)
                self.tasks += 1
            elif kind == "turn_probs":
                a.update(n=self.tasks - 1, turned=self.turned, upper=self.upper)
                two = a["t"] >= 8
                self.turned += 1 + two
                self.upper += two
            elif kind == "values":
                branch = (a["t"] >= 8) + (a["t"] >= 14)
                a.update(n=self.tasks - 1, ready=self.v_ready[branch], upper=self.upper)
            elif kind == "gain":
                a["used"] = self.gain_used
            if kind == "turn_out":
                a["n"] = self.tasks - (1 if a["t"] == 19 else 2)
                if a["t"] in (7, 13, 19):
                    self.outs_ready[(7, 13, 19).index(a["t"])] = self.misc
            if kind == "lift":
                a["outs"] = self.outs_ready[a["b"]]
            if kind in ("cumsum", "mod_sum"):
                a["after"] = self.misc
            if kind == "scores":
                a["cumsum"] = self.cumsum
            if kind == "cumsum":
                self.cumsum = self.misc
            if kind == "weigh":
                a["n"] = self.tasks - 1
            out.append((kind, unit, a))
        units = [u for _, u, _ in out if u is not None]
        ahead, at, splits = [], 0, 0
        for kind, unit, _ in [(None, None, None)] + out:
            splits += unit is not None and unit.mod is None
            now = []
            while at < len(units):
                u = units[at]
                ahead_of = u.mod is None and units_split(units, at) > splits + 1
                if ahead_of:
                    break
                now.append(u)
                at += 1
            ahead.append(now)
        self.segments[name] = (ahead[0], [(*o, ahead[i + 1]) for i, o in enumerate(out)])
        self.units[name] = units
        return out


def plain_part(part, n):
    return not (part == 0 and n >= 2 or part == 2 and n < 2)


def units_split(units, at):
    return sum(u.mod is None for u in units[:at])


def trunk(nc, x_in, c, norm_mix_g, norm_ffn_g, w_mod, b_mod, w_in, b_forget, lam_q1, lam_k1, lam_q2, lam_k2,
          subln_g, rel_bias, w_br_a, w_br_b, w_br_c, w_out, w_ff_gate, w_ff_up, w_ff_down, w_router,
          w_exp_gate, w_exp_up, w_exp_down, final_norm_g, buckets, blocked, out):
    w = dict(w_mod=w_mod, w_in=w_in, w_br_a=w_br_a, w_br_b=w_br_b, w_br_c=w_br_c, w_out=w_out)
    plan = Plan(w)
    FB = D_FF // P
    wg = w_ff_gate[0].rearrange("(kb p) n -> p kb n", p=P)
    wu = w_ff_up[0].rearrange("(kb p) n -> p kb n", p=P)
    wd = w_ff_down[0].rearrange("(fb p) n -> p fb n", p=P)
    DENSE_LOOPS = (FB - 2) // 2
    dense_raw0, dense_split0 = plan.raw_n, plan.split_n
    assert all(o == ("split", dense_split0 - R + (k - dense_raw0) % R) for k, o in
               ((k, plan.owner[k % R]) for k in range(dense_raw0, dense_raw0 + R)))
    plan.raw_n += 3 * FB
    plan.split_n += 3 * FB
    for k in range(plan.raw_n - R, plan.raw_n):
        plan.owner[k % R] = ("split", plan.split_n - plan.raw_n + k)
    plan.segment("mix1", mixer_ops(1, w))
    gains = dict(norm_mix_g=norm_mix_g, norm_ffn_g=norm_ffn_g, final_norm_g=final_norm_g)

    with ExitStack() as ctx:
        at = [nc.sbuf_base // 32 * 32 + 32]

        def place(name, shape, dt=F32, where=None):
            size = 4 * int(np.prod(shape[1:]))
            size = (size + 31) // 32 * 32
            offset = at[0] if where is None else where
            t = nc.alloc_sbuf_tensor_at(name, shape, dt, offset=offset)
            assert offset + size <= nc.sbuf_usable_end, (name, offset, size)
            if where is None:
                at[0] += size
            return t

        x = place("x", [P, NT, D])
        mod = place("mod", [P, 3, 2 * D])
        gain = place("gain", [P, D])
        ident = place("ident", [P, P])
        ident_r = place("ident_r", [P, P], F32R)
        ones = place("ones", [P, P])
        anti = place("anti", [P, P])
        neg_ident = place("neg_ident", [P, 8])
        one_hot = ident
        tri = place("tri", [P, NT, S])
        cond = place("cond", [P, KB])
        cs = place("cs", [P, KB])
        lam_s = place("lam_s", [P, DEPTH, 4])
        neg_lam = place("neg_lam", [P, DEPTH])
        subg = place("subg", [P, DEPTH, 2 * HD])
        bf = place("bf", [P, DEPTH, C_HEADS])
        wf = place("wf", [P, DEPTH, KB, C_HEADS])
        wf_hi = place("wf_hi", [P, DEPTH, KB, C_HEADS], F32R)
        wf_lo = place("wf_lo", [P, DEPTH, KB, C_HEADS], F32R)
        wr = place("wr", [P, KB, NE])
        wr_hi = place("wr_hi", [P, KB, NE], F32R)
        wr_lo = place("wr_lo", [P, KB, NE], F32R)
        stat = place("stat", [P, 64])
        lf = place("lf", [P, NT, C_HEADS])
        lf_t = place("lf_t", [P, 3, NT, C_HEADS])
        ft = place("ft", [C_HEADS, S])
        ht_at = at[0]
        ht_hi = place("ht_hi", [P, KB, S], F32R)
        ht_lo = place("ht_lo", [P, KB, S], F32R)
        merged = place("merged", [P, NT, D])
        htok = merged
        zero_r = place("zero_r", [P, P], F32R)
        arena = at[0]
        raw = place("raw", [P, R, UM])
        w_hi = place("w_hi", [P, H, UM], F32R)
        w_lo = place("w_lo", [P, H, UM], F32R)
        arena2 = at[0]
        bias = place("bias", [P, N_BIAS + 1, S])
        qkt = place("qkt", [P, 2, 6, S])
        vals = place("vals", [P, NT, VW])
        arena3 = at[0]
        prob = place("prob", [P, 2, 3 * S])
        prob_t = place("prob_t", [P, 2, 3 * S])
        o_tok = place("o_tok", [P, 2, P])
        ot_hi = place("ot_hi", [P, OW, S], F32R)
        ot_lo = place("ot_lo", [P, OW, S], F32R)
        tanh_g = place("tanh_g", [P, NT, 512], where=arena2)
        lifted = place("lifted", [P, 512], where=arena2 + 4 * NT * 512)
        rel = place("rel", [N_BUCKETS, N_BIAS + 1], where=arena3)
        buck = place("buck", [N_BUCKETS, NJ], where=arena3 + 128)
        block_sb = place("block_sb", [N_BIAS + 1, NJ], where=arena3 + 128 + 4 * NJ)
        vec = place("vec", [N_BIAS + 1, NJ], where=arena3 + 128 + 8 * NJ)
        lamv = place("lamv", [P, DEPTH, 4, HD], where=arena3 + 128 + 12 * NJ)
        lam_junk = place("lam_junk", [P, HD], where=arena3 + 128 + 12 * NJ + 32 * HD)
        silu_g = place("silu_g", [P, 2, S], where=arena3)
        act_t = place("act_t", [P, 2, S], where=arena3 + 8 * S)
        act_hi = place("act_hi", [P, 2, S], F32R, where=arena3 + 16 * S)
        act_lo = place("act_lo", [P, 2, S], F32R, where=arena3 + 24 * S)
        upd = place("upd", [P, 512], where=arena3 + 32 * S)
        e_hi = place("e_hi", [P, HE, UM], F32R, where=arena)
        e_lo = place("e_lo", [P, HE, UM], F32R, where=arena + 4 * HE * UM)
        assert arena + 8 * HE * UM <= arena2
        e_raw = place("e_raw", [P, RE, UM], where=arena3 - 4 * RE * UM)
        assert arena3 - 4 * RE * UM >= arena2 + 4 * (NT + 1) * 512
        e_at = [arena3]

        def eplace(name, shape, dt=F32):
            t = place(name, shape, dt, where=e_at[0])
            e_at[0] += (4 * int(np.prod(shape[1:])) + 31) // 32 * 32
            return t

        hh = eplace("hh", [P, NT, D], F32R)
        hl = eplace("hl", [P, NT, D], F32R)
        y_hi = eplace("y_hi", [P, D], F32R)
        y_lo = eplace("y_lo", [P, D], F32R)
        moe = merged
        xg_hi = place("xg_hi", [P, KB, P], F32R, where=ht_at)
        xg_lo = place("xg_lo", [P, KB, P], F32R, where=ht_at + 4 * KB * P)
        h_e = place("h_e", [P, CH], where=ht_at + 8 * KB * P)
        silu_e = place("silu_e", [P, CH], where=ht_at + 8 * KB * P + 4 * CH)
        he_hi = place("he_hi", [P, 4, P], F32R, where=ht_at + 8 * KB * P + 8 * CH)
        he_lo = place("he_lo", [P, 4, P], F32R, where=ht_at + 8 * KB * P + 12 * CH)
        pick = eplace("pick", [P, NT, P], F32R)
        pick_t = eplace("pick_t", [P, NT, P], F32R)
        iota_s = eplace("iota_s", [P, 2, P])
        route = eplace("route", [P, 8, NT, NE])
        top_v = eplace("top_v", [P, NT, 8])
        top_i = eplace("top_i", [P, NT, 8], U32)
        top_f = eplace("top_f", [P, NT, 8])
        table = eplace("table", [P, 3, NT, NE + 2])
        counts = eplace("counts", [P, NE])
        flag = eplace("flag", [P, 1], I32)
        flag_f = eplace("flag_f", [P, 1])
        assert e_at[0] <= nc.sbuf_usable_end

        ps = ctx.enter_context(nc.psum_tensor("ps", [P, 8, 512], F32))
        scratch = nc.dram_tensor("bias_rows", [N_BIAS + 1, NJ], F32, kind="Internal").ap()
        kept = nc.dram_tensor("bias_of_a", [P, 2 * A_HEADS, S], F32, kind="Internal").ap()
        bias_flat = bias[:].rearrange("p m k -> p (m k)")
        FLIPS = -(-(N_BIAS + 1) // 2)

        def sem(name):
            return ctx.enter_context(nc.semaphore(name))

        consts_landed = sem("consts_landed")
        consts_made = sem("consts_made")
        rel_cleared = sem("rel_cleared")
        ident_r_made = sem("ident_r_made")
        consts_split_hi = sem("consts_split_hi")
        consts_split_lo = sem("consts_split_lo")
        bias_prod = sem("bias_prod")
        bias_rows = sem("bias_rows")
        bias_landed = sem("bias_landed")
        flip_mm = sem("flip_mm")
        flip_read = sem("flip_read")
        bias_kept = sem("bias_kept")
        bias_back = sem("bias_back")
        x_landed = sem("x_landed")
        cs_ready = sem("cs_ready")
        lam_sum = sem("lam_sum")
        lam_exp = sem("lam_exp")
        lam_ready = sem("lam_ready")
        gain_landed = sem("gain_landed")
        high_done = sem("high_done")
        low_done = sem("low_done")
        units_done = sem("units_done")
        mod_used = sem("mod_used")
        mod_zero = sem("mod_zero")
        mod_mm = sem("mod_mm")
        misc_read = sem("misc_read")
        sq_done = sem("sq_done")
        h_ready = sem("h_ready")
        h_final = sem("h_final")
        e_xlow_a = sem("e_xlow_a")
        e_pick_a = sem("e_pick_a")
        merged_done = sem("merged_done")
        logits_gap = sem("logits_gap")
        turned = sem("turned")
        ht_high = sem("ht_high")
        ht_low = sem("ht_low")
        forget_mm = sem("forget_mm")
        forget_pre = sem("forget_pre")
        forget_exp = sem("forget_exp")
        forget_ln = sem("forget_ln")
        forget_log = sem("forget_log")
        cum_mm = sem("cum_mm")
        scores_done = sem("scores_done")
        biased = sem("biased")
        exp_done = sem("exp_done")
        diff_done = sem("diff_done")
        probs_turned = sem("probs_turned")
        pt_low = sem("pt_low")
        pt_up = sem("pt_up")
        values_done = sem("values_done")
        o_ready = sem("o_ready")
        sub_sum = sem("sub_sum")
        out_turned = sem("out_turned")
        ot_high = sem("ot_high")
        x_ready = sem("x_ready")
        d_silu = sem("d_silu")
        d_prod = sem("d_prod")
        d_high = sem("d_high")
        d_low = sem("d_low")
        router_mm = sem("router_mm")
        logits_read = sem("logits_read")
        route_exp_in = sem("route_exp_in")
        route_exp = sem("route_exp")
        member_done = sem("member_done")
        rank_mm = sem("rank_mm")
        table_done = sem("table_done")
        flag_done = sem("flag_done")
        hh_done = sem("hh_done")
        hl_done = sem("hl_done")
        e_consts = sem("e_consts")
        e_high = sem("e_high")
        e_low = sem("e_low")
        e_used = sem("e_used")
        e_silu = sem("e_silu")
        e_prod = sem("e_prod")
        e_turned = sem("e_turned")
        e_hhigh = sem("e_hhigh")
        e_hlow = sem("e_hlow")
        e_pick = sem("e_pick")
        e_gather = sem("e_gather")
        e_xhigh = sem("e_xhigh")
        e_xlow = sem("e_xlow")
        e_yhigh = sem("e_yhigh")
        e_ylow = sem("e_ylow")
        e_back = sem("e_back")
        e_back_read = sem("e_back_read")
        e_pick_turned = sem("e_pick_turned")
        y_cleared = sem("y_cleared")
        store_done = sem("store_done")
        out_ready = sem("out_ready")
        final_sq = sem("final_sq")
        dve_step = sem("dve_step")
        raw_landed = [sem(f"raw_landed{i}") for i in range(R)]
        e_landed = [sem(f"e_landed{i}") for i in range(RE)]
        mod_start = [[sem(f"mod_start{l}{part}") for part in range(3)] for l in range(DEPTH)]
        bank_read = [sem("bank0_read"), sem("bank1_read")]

        block = ctx.enter_context(nc.Block())
        tasks = [(p, i) for p in range(10) for i in range(NT)]
        def flat_scores(half):
            return ps[:, 2 + 2 * half:4 + 2 * half, :].rearrange("p b n -> p (b n)")

        def dense_index(f, what):
            return {"gate": 3 * f - (f > 0), "up": 3 * f + (f == 0), "down": 3 * f + 4 - 2 * (f == FB - 1)}[what]

        N_LOADS = 11 + 4 * DEPTH
        EU = 12 * NC
        LEAD = 3
        SQ, RS, DEN, NMAX, SS, SR, RDEN, COEF = 0, 2, 4, 6, 8, 10, 12, 14
        SH1, A1, G1, SH2, A2, G2 = [mod[:, k // 2, (k % 2) * D:(k % 2 + 1) * D] for k in range(6)]

        def maps(pair):
            return 3 if 4 <= pair < 7 else 1

        def bias_of(pair, half):
            if pair < 4:
                return 2 * pair + half
            if pair < 7:
                return 2 * A_HEADS + 3 * (2 * (pair - 4) + half)
            return N_BIAS

        def unit_view(ring, slot, u):
            n, width = u.shape
            return ring[:, slot, 0:n * width].rearrange("p (k n) -> p k n", k=n)

        def by_map(buf, n, i):
            return buf[:, 0:n * S].rearrange("p (m k) -> p m k", m=n)[:, :, 0:(i + 1) * P]

        def dense_slots(k):
            r, s = dense_raw0 + k, dense_split0 + k
            return r % R, s % H, r // R, s

        def expert_src(e, c, j):
            one = bass.ds(e, 1)
            if j < 8:
                view = (w_exp_gate, w_exp_up)[j // 4][0].rearrange("e (kb p) n -> e p kb n", p=P)
                src = view[one, :, 2 * (j % 4):2 * (j % 4) + 2, bass.ds(c * CH, CH)]
            else:
                view = w_exp_down[0].rearrange("e (fb p) n -> e p fb n", p=P)
                src = view[one, :, bass.ds((c - 1) * 4 + j - 8, 1), :]
            return src.rearrange("a p k n -> p (a k) n")

        BACK = (5, 6, 7, 2)

        def round_unit(c, j):
            return c * 12 + (j if isinstance(c, int) and c == 0 else j - 4)

        @block.sync
        def _(sp):
            def load_segment(name):
                for kind, u, a, _ in plan.segments[name][1]:
                    if kind == "gain":
                        if a["used"] is not None:
                            sp.wait_ge(misc_read, a["used"])
                        src = gains[a["src"]]
                        src = src[a["l"]] if a["src"] != "final_norm_g" else src
                        sp.dma_start(gain[:], src.partition_broadcast(P)).then_inc(gain_landed, 16)
                    elif u is not None:
                        if u.waits is not None:
                            sp.wait_ge(low_done if u.waits[0] == "split" else mod_used, u.waits[1] + 1)
                        sp.dma_start(unit_view(raw, u.raw, u), u.src).then_inc(raw_landed[u.raw], 16)

            def dense(k, src, nk, it=0):
                slot, _, _, s = dense_slots(k)
                sp.wait_ge(low_done, it * 6 + s - R + 1)
                sp.dma_start(raw[:, slot, :].rearrange("p (k n) -> p k n", k=nk), src)\
                    .then_inc(raw_landed[slot], 16)

            load_segment("start")
            load_segment("mix0")
            dense(0, wg[:, :, 0:P], KB)
            dense(1, wu[:, :, 0:P], KB)
            with sp.Fori(0, DENSE_LOOPS) as it:
                for f in range(2):
                    dense(2 + 3 * f, wg[:, :, bass.ds((it * 2 + 1 + f) * P, P)], KB, it)
                    dense(3 + 3 * f, wu[:, :, bass.ds((it * 2 + 1 + f) * P, P)], KB, it)
                    dense(4 + 3 * f, wd[:, bass.ds(it * 2 + f, 1), :], 1, it)
            k = 2 + 6 * DENSE_LOOPS
            dense(k, wg[:, :, (FB - 1) * P:FB * P], KB)
            dense(k + 1, wu[:, :, (FB - 1) * P:FB * P], KB)
            dense(k + 2, wd[:, FB - 2:FB - 1, :], 1)
            dense(k + 3, wd[:, FB - 1:FB, :], 1)
            load_segment("mix1")

            sp.wait_ge(values_done, len(tasks) * DEPTH)

            def expert_unit(e, c, j, base, kind=None):
                kind = j if kind is None else kind
                slot = (j if isinstance(c, int) and c == 0 else j - 4) % RE
                k = e * EU + round_unit(c, j) + base
                if not isinstance(k, int) or k >= RE:
                    sp.wait_ge(e_low, k - RE + 1)
                sp.dma_start(e_raw[:, slot, :].rearrange("p (k n) -> p k n", k=2 if kind < 8 else 1),
                             expert_src(e, c, kind)).then_inc(e_landed[slot], 16)

            def expert(e, base):
                first = isinstance(e, int) and base == 0
                for j in range(8):
                    expert_unit(e, 0, j, base)
                if first:
                    for j in range(12):
                        expert_unit(e, 1, j, base)
                with sp.Fori(1 + first, NC) as c:
                    for j in range(12):
                        expert_unit(e, c, j, base)
                for j in range(4):
                    expert_unit(e, NC, j, base, kind=8 + j)

            expert(0, 0)
            with sp.Fori(1, NE) as e:
                expert(e, 0)
            sp.wait_ge(flag_done, 1)
            more = sp.value_load(flag[0:1, 0:1], min_val=0, max_val=1)
            with sp.If(more > 0):
                with sp.Fori(0, NE) as e:
                    expert(e, NE * EU)
            sp.wait_ge(out_ready, 1)
            sp.dma_start(out[0].rearrange("(i p) d -> p i d", p=P), x[:]).then_inc(store_done, 16)
            sp.wait_ge(store_done, 16)

        @block.gpsimd
        def _(pool):
            g = nc.gpsimd
            pool.dma_start(x[:], x_in[0].rearrange("(i p) d -> p i d", p=P)).then_inc(x_landed, 16)
            g.memset(rel[:], 0.0).then_inc(rel_cleared, 1)
            def mod_begin(l, part, n):
                g.memset(mod[:, part, :], 0.0).then_inc(mod_zero, 1)
                pool.wait_ge(mod_zero, n + 1)
                pool.dma_start(mod[0:1, part, :], b_mod[l:l + 1, part * 2 * D:(part + 1) * 2 * D])\
                    .then_inc(mod_start[l][part], 16)

            mod_begin(0, 0, 0)
            g.memset(ones[:], 1.0).then_inc(consts_made, 1)
            g.memset(ident[:], 0.0).then_inc(consts_made, 1)
            g.memset(neg_ident[:], 0.0).then_inc(consts_made, 1)
            g.memset(tri[:], 1.0).then_inc(consts_made, 1)
            g.memset(zero_r[:].bitcast(F32), 0.0).then_inc(consts_made, 1)
            g.memset(anti[:], 0.0).then_inc(consts_made, 1)
            pool.wait_ge(consts_made, 6)
            g.affine_select(out=anti[:], in_=anti[:], compare_op=ALU.not_equal, fill=1.0, base=-(P - 1),
                            pattern=[[1, P]], channel_multiplier=1).then_inc(consts_made, 1)
            g.affine_select(out=ident[:], in_=ident[:], compare_op=ALU.not_equal, fill=1.0, base=0,
                            pattern=[[-1, P]], channel_multiplier=1).then_inc(consts_made, 1)
            g.affine_select(out=neg_ident[:], in_=neg_ident[:], compare_op=ALU.not_equal, fill=-1.0, base=0,
                            pattern=[[-1, 8]], channel_multiplier=1).then_inc(consts_made, 1)
            g.affine_select(out=tri[:], in_=tri[:], compare_op=ALU.is_ge, fill=0.0, base=0,
                            pattern=[[-P, NT], [1, S]], channel_multiplier=-1).then_inc(consts_made, 1)
            mod_begin(0, 1, 1)
            mod_begin(0, 2, 2)
            for l in range(DEPTH):
                if l == 0:
                    pool.wait_ge(h_ready, 2)
                    mod_begin(1, 0, 3)
                else:
                    pool.wait_ge(x_ready, 2)
                    mod_begin(1, 1, 4)
                    mod_begin(1, 2, 5)
            pool.wait_ge(hl_done, 1)
            pool.wait_ge(turned, 24)
            g.iota(iota_s[:], pattern=[[P, 2], [1, P]], base=0, channel_multiplier=0,
                   allow_small_or_imprecise_dtypes=True).then_inc(e_consts, 1)
            g.memset(pick_t[:].bitcast(F32), 0.0).then_inc(e_consts, 1)
            g.memset(table[:], 0.0).then_inc(e_consts, 1)
            g.memset(moe[:], 0.0).then_inc(e_consts, 1)

        @block.scalar
        def _(act):
            copy = ACT.Copy
            A = nc.scalar.activation
            loads = [
                (cond[:], c[0].rearrange("(kb p) -> p kb", p=P)),
                (subg[:, 0, :], subln_g[0].partition_broadcast(P)),
                (subg[:, 1, :], subln_g[1].partition_broadcast(P)),
                (bf[:, 0, :], b_forget[0].partition_broadcast(P)),
                (bf[:, 1, :], b_forget[1].partition_broadcast(P)),
                (wf[:, 0], w_in[0, :, FC:GC].rearrange("(kb p) n -> p kb n", p=P)),
                (wf[:, 1], w_in[1, :, FC:GC].rearrange("(kb p) n -> p kb n", p=P)),
                (wr[:], w_router[0].rearrange("(kb p) n -> p kb n", p=P)),
                (buck[:], buckets), (block_sb[:], blocked),
            ]
            loads += [(lamv[:, l, k, :], v[l].partition_broadcast(P))
                      for l in range(DEPTH) for k, v in enumerate((lam_q1, lam_k1, lam_q2, lam_k2))]
            act.wait_ge(rel_cleared, 1)
            loads.append((rel[:, 0:N_BIAS], rel_bias))
            with nc.allow_non_contiguous_dma(reason="a few small parameters"):
                for dst, src in loads:
                    act.dma_start(dst, src).then_inc(consts_landed, 16)
            act.wait_ge(consts_landed, 16 * len(loads))
            A(cs[:], cond[:], ACT.Silu).then_inc(cs_ready, 1)
            A(wf_hi[:], wf[:], copy).then_inc(consts_split_hi, 1)
            A(wr_hi[:], wr[:], copy).then_inc(consts_split_hi, 1)
            act.wait_ge(consts_made, 10)
            A(ident_r[:], ident[:], copy).then_inc(ident_r_made, 1)
            act.wait_ge(lam_sum, 4)
            A(lam_s[:, :, 2:4], lam_s[:, :, 0:2], ACT.Exp).then_inc(lam_exp, 1)
            act.wait_ge(misc_read, 1)
            act.dma_start(scratch, vec[:]).then_inc(bias_rows, 16)
            act.wait_ge(bias_rows, 16)

            def toeplitz(row, count):
                return bass.AP(scratch.tensor, row * NJ, [[1, P], [NJ, count], [1, S]])

            act.dma_start(bias[:, 0:2 * A_HEADS, :], toeplitz(0, 2 * A_HEADS)).then_inc(bias_landed, 16)
            for gr in range(G):
                r = 2 * A_HEADS
                act.dma_start(bias[:, r + gr:r + G * B_HEADS:G, :], toeplitz(r + gr * B_HEADS, B_HEADS))\
                    .then_inc(bias_landed, 16)
            act.dma_start(bias[:, N_BIAS:N_BIAS + 1, :], toeplitz(N_BIAS, 1)).then_inc(bias_landed, 16)
            for n in range(FLIPS):
                act.wait_ge(flip_mm, n + 1)
                w_ = min(2 * S, (N_BIAS + 1) * S - n * 2 * S)
                A(bias_flat[:, n * 2 * S:n * 2 * S + w_], ps[:, n % 6, 0:w_], copy).then_inc(flip_read, 1)
            act.wait_ge(flip_read, FLIPS)
            act.dma_start(kept, bias[:, 0:2 * A_HEADS, :]).then_inc(bias_kept, 16)

            def squares(n):
                for i in range(NT):
                    A(htok[:, i, :], x[:, i, :], ACT.Square, accum_out=stat[:, SQ + i:SQ + i + 1]).then_inc(sq_done, 1)

            def turn_high(k, scale=1.0):
                for n in range(4):
                    i, half = n // 2, n % 2
                    act.wait_ge(turned, 4 * k + n + 1)
                    A(ht_hi[:, 4 * half:4 * half + 4, i * P:(i + 1) * P],
                      ps[:, 2 + n, :].rearrange("p (k t) -> p k t", k=4), copy, scale=scale).then_inc(ht_high, 1)

            def copy_part(a):
                n = a["n"]
                if plain_part(a["part"], n):
                    act.wait_ge(mod_mm, a["nth"] + 1)
                    A(mod[:, a["part"], n * 512:(n + 1) * 512], ps[:, 7, :], copy).then_inc(misc_read, 1)

            def high(u):
                act.wait_ge(raw_landed[u.raw], u.landed)
                if u.split >= H:
                    act.wait_ge(units_done, u.split - H + 1)
                A(unit_view(w_hi, u.hl, u), unit_view(raw, u.raw, u), copy).then_inc(high_done, 1)

            def mixer(l):
                first, ops = plan.segments[f"mix{l}"]
                for u in first:
                    if u.mod is None:
                        high(u)
                for kind, unit, a, ahead in ops:
                    for u in ahead:
                        if u.mod is None:
                            high(u)
                    if kind == "qk":
                        b, j, pair = a["bank"], a["j"], a["pair"]
                        if pair >= 2:
                            act.wait_ge(scores_done, len(tasks) * l + 2 * (pair - 1))
                        act.wait_ge(units_done, unit.split + 1)
                        A(qkt[:, pair % 2, j, :], ps[:, b, 0:S], copy, scale=HD ** -0.5 if j < 3 else 1.0)\
                            .then_inc(bank_read[b], 1)
                    elif kind == "v" and a["last"]:
                        act.wait_ge(units_done, unit.split + 1)
                        for i in range(NT):
                            A(vals[:, i, a["dst"]:a["dst"] + a["width"]], ps[:, i, 0:a["width"]], copy)\
                                .then_inc(bank_read[i], 1)
                    elif kind == "gate" and a["last"]:
                        act.wait_ge(units_done, unit.split + 1)
                        for i in range(NT):
                            A(tanh_g[:, i, :], ps[:, i, :], ACT.Tanh, scale=0.5).then_inc(bank_read[i], 1)
                    elif kind == "forget":
                        act.wait_ge(forget_pre, l + 1)
                        A(lf_t[:, 2], lf_t[:, 1], ACT.Exp, scale=-1.0).then_inc(forget_exp, 1)
                        act.wait_ge(forget_exp, l + 1)
                        A(lf_t[:, 2], lf_t[:, 2], ACT.Ln, bias=1.0).then_inc(forget_ln, 1)
                    elif kind == "cumsum":
                        act.wait_ge(cum_mm, l + 1)
                        A(ft[:], ps[0:C_HEADS, 7, 0:S], copy).then_inc(misc_read, 1)
                    elif kind == "mod_sum":
                        copy_part(a)
                    elif kind == "scores":
                        pair, i = tasks[a["t"]]
                        for half in range(2):
                            act.wait_ge(biased, 2 * a["n"] + half + 1)
                            view = by_map(prob[:, half], maps(pair), i)
                            A(view, view, ACT.Exp, scale=-1.0, bias=stat[:, NMAX + half:NMAX + half + 1],
                              accum_out=stat[:, DEN + half:DEN + half + 1]).then_inc(exp_done, 1)
                    elif kind == "turn_probs":
                        pair, i = tasks[a["t"]]
                        if a["n"]:
                            act.wait_ge(values_done, a["n"])
                        act.wait_ge(probs_turned, a["turned"] + 1)
                        width = maps(pair) * (i + 1) * P
                        A(prob_t[:, 0, 0:width], flat_scores(0)[:, 0:width], copy).then_inc(pt_low, 1)
                    elif kind == "turn_out":
                        _, i = tasks[a["t"]]
                        act.wait_ge(out_turned, a["n"] + 1)
                        A(ot_hi[:, a["t"] // 2, i * P:(i + 1) * P], ps[:, 7, 0:P], copy).then_inc(ot_high, 1)
                    elif kind == "turn_merged":
                        turn_high(1 + 3 * l, 0.5)

            def dense_high(k, it=0, used=None):
                slot, hl, before, s = dense_slots(k)
                act.wait_ge(raw_landed[slot], it * 16 + 16 * (before + 1))
                act.wait_ge(units_done, it * 6 + s - H + 1)
                A(w_hi[:, hl, :], raw[:, slot, :], copy).then_inc(high_done, 1)

            def dense_block(f, k, it=0, more=True):
                b = f % 2
                if more:
                    dense_high(k, it)
                act.wait_ge(units_done, it * 6 + dense_split0 + dense_index(f, "gate") + 1)
                A(silu_g[:, b, :], ps[:, 4 + b, 0:S], ACT.Silu).then_inc(d_silu, 1)
                if more:
                    dense_high(k + 1, it)
                act.wait_ge(d_prod, it * 2 + f + 1)
                A(act_hi[:, b, :], act_t[:, b, :], copy).then_inc(d_high, 1)
                dense_high(k + 2 if more else k, it)

            def dense():
                dense_high(0)
                dense_high(1)
                with act.Fori(0, DENSE_LOOPS) as it:
                    dense_block(0, 2, it)
                    dense_block(1, 5, it)
                k = 2 + 6 * DENSE_LOOPS
                dense_block(FB - 2, k)
                dense_block(FB - 1, k + 3, more=False)

            def experts(n):
                e0 = n * NE

                def unit(e, c, j):
                    k = j if isinstance(c, int) and c == 0 else j - 4
                    slot, hl = k % RE, k % HE
                    lap = (e + e0) * NC + c - (slot != k)
                    act.wait_ge(e_landed[slot], (lap + 1) * 16)
                    done = (e + e0) * EU + round_unit(c, j)
                    if not isinstance(done, int) or done >= HE:
                        act.wait_ge(e_used, done - HE + 1)
                    A(e_hi[:, hl, :], e_raw[:, slot, :], copy).then_inc(e_high, 1)

                def gathered(count):
                    act.wait_ge(e_gather, count)
                    A(xg_hi[:], ps[:, 5:7, :].rearrange("p b (k t) -> p (b k) t", k=4), copy).then_inc(e_xhigh, 1)

                def hidden(count):
                    act.wait_ge(e_turned, count)
                    A(he_hi[:], ps[:, 2, :].rearrange("p (k t) -> p k t", k=4), copy).then_inc(e_hhigh, 1)

                def expert(e, fresh):
                    done = (e + e0) * EU
                    for j in range(5):
                        unit(e, 0, j)
                    if fresh:
                        act.wait_ge(y_cleared, n + 1)
                    else:
                        act.wait_ge(e_used, done)
                    A(y_hi[:], ps[:, 3:5, :].rearrange("p b n -> p (b n)"), copy).then_inc(e_yhigh, 1)
                    for j in range(5, 8):
                        unit(e, 0, j)
                    act.wait_ge(e_used, done + 4)
                    A(silu_e[:], ps[:, 0, :], ACT.Silu).then_inc(e_silu, 1)
                    for j in range(LEAD):
                        unit(e, 1, j)
                    with act.Fori(1, NC) as c:
                        for j in range(LEAD, 9):
                            unit(e, c, j)
                        act.wait_ge(e_used, done + round_unit(c, 4))
                        act.wait_ge(e_prod, (e + e0) * NC + c)
                        A(silu_e[:], ps[:, 0, :], ACT.Silu).then_inc(e_silu, 1)
                        hidden((e + e0) * NC + c)
                        for j in range(9, 12):
                            unit(e, c, j)
                        for j in range(LEAD):
                            unit(e, c + 1, j)
                    unit(e, NC, 3)
                    hidden((e + e0) * NC + NC)
                    gathered(e + e0 + n + 2)

                gathered(n * (NE + 1) + 1)
                expert(0, True)
                with act.Fori(1, NE) as e:
                    expert(e, False)
                act.wait_ge(e_used, (NE + e0) * EU)
                A(y_hi[:], ps[:, 3:5, :].rearrange("p b n -> p (b n)"), copy).then_inc(e_yhigh, 1)

            for kind, _, a, _ in plan.segments["start"][1]:
                if kind == "mod_sum":
                    copy_part(a)
            squares_ready = [(x_landed, 16), (x_ready, 1), (x_ready, 2), (x_ready, 3)]
            for n, k in ((0, 0), (1, 2)):
                act.wait_ge(*squares_ready[n])
                squares(n)
                turn_high(k)
                if not n:
                    act.wait_ge(bias_kept, 16)
                else:
                    act.dma_start(bias[:, 0:2 * A_HEADS, :], kept).then_inc(bias_back, 16)
                mixer(0) if n == 0 else dense()
            for n, k in ((2, 3), (3, 5)):
                act.wait_ge(*squares_ready[n])
                squares(n)
                turn_high(k)
                if n == 2:
                    mixer(1)
            act.wait_ge(h_ready, 8)
            A(hh[:], htok[:], copy).then_inc(hh_done, 1)
            act.wait_ge(route_exp_in, 1)
            A(route[:, 0, :, 1:2], route[:, 0, :, 0:1], ACT.Exp).then_inc(route_exp, 1)
            act.wait_ge(units_done, plan.split_n)
            act.wait_ge(low_done, plan.split_n)
            experts(0)
            act.wait_ge(flag_done, 1)
            more = act.value_load(flag[0:1, 0:1], min_val=0, max_val=1)
            with act.If(more > 0):
                experts(1)
            act.wait_ge(h_final, 1)
            for i in range(NT):
                A(moe[:, i, :], x[:, i, :], ACT.Square, accum_out=stat[:, SQ + i:SQ + i + 1]).then_inc(final_sq, 1)

        @block.tensor
        def _(pe):
            mm = pe.matmul

            def product(dst, lhs, rhs, start, stop):
                mm(dst, lhs[0], rhs[0], start=start, stop=False)
                mm(dst, lhs[0], rhs[1], start=False, stop=False)
                return mm(dst, lhs[1], rhs[0], start=False, stop=stop)

            def pair_of(hi, lo, *at):
                return hi[at], lo[at]

            def turn(k, src):
                for n in range(4):
                    i, half = n // 2, n % 2
                    for j in range(4):
                        kb = 4 * half + j
                        last = pe.transpose(ps[:, 2 + n, j * P:(j + 1) * P], src[:, i, kb * P:(kb + 1) * P], ident[:])
                    last.then_inc(turned, 1)

            def mixer(l):
                _, ops = plan.segments[f"mix{l}"]
                pe.wait_ge(ht_low, 4 * (3 * l + 1))
                for kind, unit, a, _ in ops:
                    if unit is not None and unit.mod is None:
                        pe.wait_ge(low_done, unit.split + 1)
                        wh, wl = unit_view(w_hi, unit.hl, unit), unit_view(w_lo, unit.hl, unit)
                    if kind == "qk":
                        b = a["bank"]
                        if a["uses"]:
                            pe.wait_ge(bank_read[b], a["uses"])
                        for kb in range(KB):
                            last = product(ps[:, b, 0:S], (wh[:, kb, :], wl[:, kb, :]),
                                           (ht_hi[:, kb, :], ht_lo[:, kb, :]), kb == 0, kb == KB - 1)
                        last.then_inc(units_done, 1)
                    elif kind in ("v", "gate", "lift", "out"):
                        off, hi, lo = 0, ht_hi, ht_lo
                        if kind == "lift":
                            off, hi, lo = (0, 4, 7)[a["b"]], ot_hi, ot_lo
                        if a["first"]:
                            for i in range(NT):
                                if a["uses"][i]:
                                    pe.wait_ge(bank_read[i], a["uses"][i])
                            if kind == "lift":
                                pe.wait_ge(misc_read, a["outs"])
                            if kind == "out" and a["n"] == 0:
                                pe.wait_ge(ht_low, 4 * (3 * l + 2))
                        nk, width = unit.shape
                        for k in range(nk):
                            for i in range(NT):
                                tok = slice(i * P, (i + 1) * P)
                                last = product(ps[:, i, 0:width],
                                               (hi[:, off + a["k0"] + k, tok], lo[:, off + a["k0"] + k, tok]),
                                               (wh[:, k, :], wl[:, k, :]), a["first"] and k == 0,
                                               a["last"] and k == nk - 1)
                        last.then_inc(units_done, 1)
                    elif kind == "forget":
                        pe.wait_ge(misc_read, a["misc"])
                        pe.wait_ge(consts_split_lo, 2)
                        for i in range(NT):
                            for kb in range(KB):
                                tok = slice(i * P, (i + 1) * P)
                                last = product(ps[:, 7, 8 * i:8 * i + C_HEADS], (ht_hi[:, kb, tok], ht_lo[:, kb, tok]),
                                               (wf_hi[:, l, kb, :], wf_lo[:, l, kb, :]), kb == 0, kb == KB - 1)
                        last.then_inc(forget_mm, 1)
                    elif kind == "cumsum":
                        pe.wait_ge(misc_read, a["misc"])
                        pe.wait_ge(forget_log, l + 1)
                        for i in range(NT):
                            last = mm(ps[0:C_HEADS, 7, 0:S], lf[:, i, :], tri[:, i, :], start=i == 0, stop=i == NT - 1)
                        last.then_inc(cum_mm, 1)
                    elif kind == "mod_sum":
                        sum_part(a)
                    elif kind == "scores":
                        pair, i = tasks[a["t"]]
                        n = maps(pair)
                        for b in range(2):
                            pe.wait_ge(bank_read[b], a["ready"][b])
                        if a["n"]:
                            pe.wait_ge(biased, 2 * a["n"])
                            pe.wait_ge(pt_low, a["n"])
                            if a["upper"]:
                                pe.wait_ge(pt_up, a["upper"])
                        if pair >= 7:
                            pe.wait_ge(misc_read, a["cumsum"])
                        K = (i + 1) * P
                        for half in range(2):
                            rows = slice(HD * half, HD * (half + 1))
                            for m in range(n):
                                dst = flat_scores(half)[:, m * S:m * S + K]
                                last = mm(dst, qkt[rows, pair % 2, m, i * P:(i + 1) * P],
                                          qkt[rows, pair % 2, 3 + m, 0:K], start=True, stop=pair < 7)
                        if pair >= 7:
                            for half in range(2):
                                h = 2 * (pair - 7) + half
                                dst = flat_scores(half)[:, 0:K]
                                mm(dst, ft[:, i * P:(i + 1) * P], ident[0:C_HEADS, h:h + 1].to_broadcast([C_HEADS, K]),
                                   start=False, stop=False)
                                last = mm(dst, neg_ident[0:C_HEADS, h:h + 1].to_broadcast([C_HEADS, P]), ft[:, 0:K],
                                          start=False, stop=True)
                        last.then_inc(scores_done, 1)
                    elif kind == "turn_probs":
                        pair, i = tasks[a["t"]]
                        for half in range(1 + (pair >= 4)):
                            if pair < 4:
                                pe.wait_ge(diff_done, 8 * l + a["t"] + 1)
                            else:
                                pe.wait_ge(exp_done, 2 * a["n"] + half + 1)
                            for m in range(maps(pair)):
                                for kb in range(i + 1):
                                    at_ = (m * (i + 1) + kb) * P
                                    last = pe.transpose(flat_scores(half)[:, at_:at_ + P],
                                                        prob[:, half, m * S + kb * P:m * S + (kb + 1) * P], ident[:])
                            last.then_inc(probs_turned, 1)
                    elif kind == "values":
                        pair, i = tasks[a["t"]]
                        n = maps(pair)
                        pe.wait_ge(pt_low, a["n"] + 1)
                        if pair >= 4:
                            pe.wait_ge(pt_up, a["upper"])
                        for b in range(2):
                            pe.wait_ge(bank_read[b], a["ready"][b])
                        if a["n"]:
                            pe.wait_ge(o_ready, a["n"])
                        for half in range(1 + (pair >= 4)):
                            width = P if pair < 4 else HD
                            dst = ps[:, 6, half * HD:half * HD + width]
                            steps = [(m, kb) for m in range(n) for kb in range(i + 1)]
                            for s_, (m, kb) in enumerate(steps):
                                if pair < 4:
                                    col = P * pair
                                elif pair < 7:
                                    col = A_W + m * B_W + HD * (2 * (pair - 4) + half)
                                else:
                                    col = A_W + G * B_W + HD * (2 * (pair - 7) + half)
                                at_ = (m * (i + 1) + kb) * P
                                last = mm(dst, prob_t[:, half, at_:at_ + P], vals[:, kb, col:col + width],
                                          start=s_ == 0, stop=s_ == len(steps) - 1)
                        last.then_inc(values_done, 1)
                    elif kind == "turn_out":
                        pe.wait_ge(misc_read, a["misc"])
                        pe.wait_ge(o_ready, a["n"] + 1)
                        pe.transpose(ps[:, 7, 0:P], o_tok[:, a["t"] % 2, :], ident[:]).then_inc(out_turned, 1)
                    elif kind == "turn_merged":
                        pe.wait_ge(merged_done, 12 * (l + 1))
                        turn(1 + 3 * l, merged)

            def sum_part(a):
                n = a["n"]
                pe.wait_ge(mod_used, 16 * (a["nth"] // 4 + 1))
                pe.wait_ge(misc_read, a["misc"])
                mm(ps[:, 7, :], ones[:], mod[:, a["part"], n * 512:(n + 1) * 512], start=True, stop=True)\
                    .then_inc(mod_mm, 1)

            def dense():
                pe.wait_ge(ht_low, 12)
                for n in range(4):
                    mm(ps[:, n, :], zero_r[:], ht_hi[:, 0:2, :].rearrange("p k t -> p (k t)"), start=True, stop=False)

                def up(k, f, it=0):
                    for j in range(2):
                        _, hl, _, s = dense_slots(k + j)
                        pe.wait_ge(low_done, it * 6 + s + 1)
                        if j == 0 and not (isinstance(it, int) and f < 2):
                            pe.wait_ge(d_prod, it * 2 + f - 1)
                        for kb in range(KB):
                            last = product(ps[:, 4 + 2 * j + f % 2, 0:S],
                                           (w_hi[:, hl, kb * P:(kb + 1) * P], w_lo[:, hl, kb * P:(kb + 1) * P]),
                                           (ht_hi[:, kb, :], ht_lo[:, kb, :]), kb == 0, kb == KB - 1)
                        last.then_inc(units_done, 1)

                def down(k, f, it=0, stop=False):
                    _, hl, _, s = dense_slots(k)
                    pe.wait_ge(low_done, it * 6 + s + 1)
                    pe.wait_ge(d_low, it * 2 + f + 1)
                    for i in range(NT):
                        for n in range(2):
                            tok = slice(i * P, (i + 1) * P)
                            last = product(ps[:, 2 * i + n, :], (act_hi[:, f % 2, tok], act_lo[:, f % 2, tok]),
                                           (w_hi[:, hl, n * 512:(n + 1) * 512], w_lo[:, hl, n * 512:(n + 1) * 512]),
                                           False, stop)
                    last.then_inc(units_done, 1)

                up(0, 0)
                up(2, 1)
                down(4, 0)
                up(5, 2)
                down(7, 1)
                with pe.Fori(1, DENSE_LOOPS) as it:
                    up(2, 1, it)
                    down(4, 0, it)
                    up(5, 2, it)
                    down(7, 1, it)
                k = 2 + 6 * DENSE_LOOPS
                up(k, FB - 1)
                down(k + 2, FB - 2)
                down(k + 3, FB - 1, stop=True)

            def router():
                pe.wait_ge(ht_low, 24)
                for i in range(NT):
                    for kb in range(KB):
                        tok = slice(i * P, (i + 1) * P)
                        last = product(ps[:, 7, NE * i:NE * (i + 1)], (ht_hi[:, kb, tok], ht_lo[:, kb, tok]),
                                       (wr_hi[:, kb, :], wr_lo[:, kb, :]), kb == 0, kb == KB - 1)
                last.then_inc(router_mm, 1)
                pe.wait_ge(member_done, 1)
                for i in range(NT):
                    for j in range(i + 1):
                        mm(ps[:, 7, NE * i:NE * (i + 1)], tri[:, j, i * P:(i + 1) * P], route[:, 4, j, :],
                           start=j == 0, stop=j == i)
                for j in range(NT):
                    last = mm(ps[:, 7, 2 * NE:3 * NE], ones[:], route[:, 4, j, :], start=j == 0, stop=j == NT - 1)
                last.then_inc(rank_mm, 1)

            def experts(n):
                e0 = n * NE

                def split_unit(e, c, j):
                    pe.wait_ge(e_low, (e + e0) * EU + round_unit(c, j) + 1)
                    hl = (j if isinstance(c, int) and c == 0 else j - 4) % HE
                    return e_hi[:, hl, :], e_lo[:, hl, :]

                def hidden(bank, e, c, j0):
                    for j in range(4):
                        wh, wl = split_unit(e, c, j0 + j)
                        for k in range(2):
                            kb = 2 * j + k
                            last = product(ps[:, bank, :], (xg_hi[:, kb, :], xg_lo[:, kb, :]),
                                           (wh[:, k * CH:(k + 1) * CH], wl[:, k * CH:(k + 1) * CH]),
                                           kb == 0, kb == KB - 1)
                        last.then_inc(e_used, 1)

                def turn_hidden(count):
                    pe.wait_ge(e_prod, count)
                    for j in range(4):
                        last = pe.transpose(ps[:, 2, j * P:(j + 1) * P], h_e[:, j * P:(j + 1) * P], ident[:])
                    last.then_inc(e_turned, 1)

                def down(e, c, j0, stop=False):
                    pe.wait_ge(e_hlow, (e + e0) * NC + c)
                    for j in range(4):
                        wh, wl = split_unit(e, c, j0 + j)
                        for h in range(2):
                            cols = slice(h * 512, (h + 1) * 512)
                            last = product(ps[:, 3 + h, :], (he_hi[:, j, :], he_lo[:, j, :]),
                                           (wh[:, cols], wl[:, cols]), False, stop and j == 3)
                        last.then_inc(e_used, 1)

                def gather(count):
                    pe.wait_ge(e_pick, count)
                    for part, src, banks in ((0, hh, (5, 6)), (1, hl, (7, 0))):
                        for kb in range(KB):
                            for i in range(NT):
                                last = mm(ps[:, banks[kb // 4], (kb % 4) * P:(kb % 4 + 1) * P],
                                          src[:, i, kb * P:(kb + 1) * P], pick[:, i, :], start=i == 0, stop=i == NT - 1)
                    last.then_inc(e_gather, 1)

                def scatter(count):
                    pe.wait_ge(e_ylow, count)
                    for i in range(NT):
                        for h in range(2):
                            bank = BACK[2 * i + h]
                            mm(ps[:, bank, :], pick_t[:, i, :], y_hi[:, h * 512:(h + 1) * 512], start=True, stop=False)
                            mm(ps[:, bank, :], pick_t[:, i, :], y_lo[:, h * 512:(h + 1) * 512], start=False, stop=True)\
                                .then_inc(e_back, 1)

                def turn_pick():
                    for i in range(NT):
                        last = mm(ps[:, 7, i * P:(i + 1) * P], pick[:, i, :], ident_r[:], start=True, stop=True)
                    last.then_inc(e_pick_turned, 1)

                def expert(e):
                    pe.wait_ge(e_xlow, (e + e0) + n + 1)
                    hidden(0, e, 0, 0)
                    scatter((e + e0) + n + 1)
                    for h in range(2):
                        mm(ps[:, 3 + h, :], zero_r[:], xg_hi[:, 0:4, :].rearrange("p k t -> p (k t)"), start=True, stop=False)
                    if not (isinstance(e, int) and e + e0 == 0):
                        pe.wait_ge(e_prod, (e + e0) * NC)
                    hidden(1, e, 0, 4)
                    pe.wait_ge(e_back_read, ((e + e0) + n + 1) * 4)
                    turn_pick()
                    with pe.Fori(1, NC) as c:
                        chunks = (e + e0) * NC + c
                        pe.wait_ge(e_silu, chunks)
                        hidden(0, e, c, 0)
                        turn_hidden(chunks)
                        hidden(1, e, c, 4)
                        down(e, c, 8)
                    turn_hidden((e + e0) * NC + NC)
                    pe.wait_ge(e_silu, (e + e0) * NC + NC)
                    gather((e + e0) + n + 2)
                    down(e, NC, 0, stop=True)

                gather(e0 + n + 1)
                expert(0)
                with pe.Fori(1, NE) as e:
                    expert(e)
                scatter(e0 + n + NE + 1)

            pe.wait_ge(consts_landed, 16 * N_LOADS)
            mm(ps[0:N_BIAS + 1, 7, 0:NJ], rel[:], buck[:], start=True, stop=True).then_inc(bias_prod, 1)
            pe.wait_ge(consts_made, 10)
            pe.wait_ge(bias_landed, 16 * 5)
            for n in range(FLIPS):
                if n >= 6:
                    pe.wait_ge(flip_read, n - 5)
                w_ = min(2 * S, (N_BIAS + 1) * S - n * 2 * S)
                mm(ps[:, n % 6, 0:w_], anti[:], bias_flat[:, n * 2 * S:n * 2 * S + w_], start=True, stop=True)\
                    .then_inc(flip_mm, 1)
            for kind, unit, a, _ in plan.segments["start"][1]:
                if kind == "mod_sum":
                    sum_part(a)
            pe.wait_ge(h_ready, 2)
            turn(0, htok)
            mixer(0)
            pe.wait_ge(h_ready, 4)
            turn(2, htok)
            dense()
            pe.wait_ge(h_ready, 6)
            turn(3, htok)
            mixer(1)
            pe.wait_ge(h_ready, 8)
            turn(5, htok)
            router()
            experts(0)
            pe.wait_ge(flag_done, 1)
            more = pe.value_load(flag[0:1, 0:1], min_val=0, max_val=1)
            with pe.If(more > 0):
                experts(1)

        @block.vector
        def _(dve):
            V = nc.vector
            STT, TT, TS = V.scalar_tensor_tensor, V.tensor_tensor, V.tensor_scalar
            count = [0]

            def step(ins):
                count[0] += 1
                ins.then_inc(dve_step, 1)
                dve.wait_ge(dve_step, count[0])

            def rstd(dst, src, width, size):
                y, s_ = stat[:, dst:dst + width], stat[:, src:src + width]
                a_, t = stat[:, 20:20 + width], stat[:, 22:22 + width]
                step(TS(a_, s_, 1.0 / size, EPS, ALU.mult, ALU.add))
                step(TS(t.bitcast(I32), a_.bitcast(I32), 1, None, ALU.logical_shift_right))
                step(TS(y.bitcast(I32), t.bitcast(I32), -1.0, float(0x5F3759DF), ALU.mult, ALU.add))
                step(TS(a_, a_, -0.5, None, ALU.mult))
                for _ in range(4):
                    step(TT(t, y, y, ALU.mult))
                    step(TT(t, t, a_, ALU.mult))
                    step(STT(y, t, 1.5, y, ALU.add, ALU.mult))

            def modulate(n, a_, b_):
                dve.wait_ge(sq_done, 2 * n + 2)
                rstd(RS, SQ, NT, D)
                for i in range(NT):
                    step(STT(htok[:, i, :], x[:, i, :], stat[:, RS + i:RS + i + 1], a_, ALU.mult, ALU.mult))
                    TT(htok[:, i, :], htok[:, i, :], b_, ALU.add).then_inc(h_ready, 1)

            def turn_low(k, scale=1.0):
                for n in range(4):
                    i, half = n // 2, n % 2
                    dve.wait_ge(ht_high, 4 * k + n + 1)
                    at_ = (slice(None), slice(4 * half, 4 * half + 4), slice(i * P, (i + 1) * P))
                    STT(ht_lo[at_], ps[:, 2 + n, :].rearrange("p (k t) -> p k t", k=4), scale,
                        ht_hi[at_].bitcast(F32), ALU.mult, ALU.subtract).then_inc(ht_low, 1)

            def use(u):
                if u.mod is None:
                    dve.wait_ge(high_done, u.split + 1)
                    TT(unit_view(w_lo, u.hl, u), unit_view(raw, u.raw, u), unit_view(w_hi, u.hl, u).bitcast(F32),
                       ALU.subtract).then_inc(low_done, 1)
                    return
                l, part, kb, half = u.mod
                dve.wait_ge(raw_landed[u.raw], u.landed)
                if kb == 0 and half == 0:
                    dve.wait_ge(mod_start[l][part], 16)
                if kb:
                    dve.wait_ge(mod_used, u.nth - 1)
                acc = mod[:, part, half * UM:(half + 1) * UM]
                STT(acc, raw[:, u.raw, :], cs[:, kb:kb + 1], acc, ALU.mult, ALU.add).then_inc(mod_used, 1)

            def scale_part(a):
                n = a["n"]
                if not plain_part(a["part"], n):
                    dve.wait_ge(gain_landed, 16 * (2 * a["l"] + (a["part"] == 2) + 1))
                    dve.wait_ge(mod_mm, a["nth"] + 1)
                    STT(mod[:, a["part"], n * 512:(n + 1) * 512], ps[:, 7, :], 1.0,
                        gain[:, (n % 2) * 512:(n % 2 + 1) * 512], ALU.add, ALU.mult).then_inc(misc_read, 1)

            def mixer(l):
                first, ops = plan.segments[f"mix{l}"]
                for u in first:
                    use(u)
                for kind, unit, a, ahead in ops:
                    for u in ahead:
                        use(u)
                    if kind == "forget":
                        dve.wait_ge(forget_mm, l + 1)
                        for i in range(NT):
                            z = TT(lf_t[:, 0, i, :], ps[:, 7, 8 * i:8 * i + C_HEADS], bf[:, l, :], ALU.add)
                            z.then_inc(misc_read, 1) if i == NT - 1 else step(z)
                        dve.wait_ge(misc_read, a["misc"] + 1)
                        STT(lf_t[:, 1], lf_t[:, 0], -1.0, lf_t[:, 0], ALU.mult, ALU.max).then_inc(forget_pre, 1)
                        dve.wait_ge(forget_ln, l + 1)
                        STT(lf[:], lf_t[:, 0], 0.0, lf_t[:, 2], ALU.min, ALU.subtract).then_inc(forget_log, 1)
                    elif kind == "mod_sum":
                        scale_part(a)
                    elif kind == "scores":
                        pair, i = tasks[a["t"]]
                        n = maps(pair)
                        dve.wait_ge(scores_done, a["n"] + 1)
                        if a["t"] == 0:
                            dve.wait_ge(flip_read, FLIPS)
                            if l:
                                dve.wait_ge(bias_back, 16)
                        for half in range(2):
                            r = bias_of(pair, half)
                            V.tensor_tensor_reduce(by_map(prob[:, half], n, i), by_map(flat_scores(half), n, i),
                                                   bias[:, r:r + n, P * (1 - i):S], -1.0, 3e38, ALU.add, ALU.min,
                                                   stat[:, NMAX + half:NMAX + half + 1]).then_inc(biased, 1)
                    elif kind == "weigh":
                        pair, i = tasks[a["t"]]
                        dve.wait_ge(exp_done, 2 * a["n"] + 2)
                        step(V.reciprocal(stat[:, RDEN:RDEN + 2], stat[:, DEN:DEN + 2]))
                        if pair < 4:
                            step(STT(stat[:, COEF:COEF + 1], stat[:, DEN:DEN + 1], stat[:, RDEN + 1:RDEN + 2],
                                     neg_lam[:, l:l + 1], ALU.mult, ALU.mult))
                            K = (i + 1) * P
                            STT(prob[:, 0, 0:K], prob[:, 1, 0:K], stat[:, COEF:COEF + 1], prob[:, 0, 0:K],
                                ALU.mult, ALU.add).then_inc(diff_done, 1)
                    elif kind == "turn_probs":
                        pair, i = tasks[a["t"]]
                        if pair >= 4:
                            if a["n"]:
                                dve.wait_ge(values_done, a["n"])
                            dve.wait_ge(probs_turned, a["turned"] + 2)
                            width = maps(pair) * (i + 1) * P
                            V.tensor_copy(prob_t[:, 1, 0:width], flat_scores(1)[:, 0:width]).then_inc(pt_up, 1)
                    elif kind == "values":
                        pair, i = tasks[a["t"]]
                        o = o_tok[:, a["t"] % 2, :]
                        dve.wait_ge(values_done, a["n"] + 1)
                        if pair < 4:
                            step(TS(o, ps[:, 6, 0:P], stat[:, RDEN:RDEN + 1], None, ALU.mult))
                            V.tensor_tensor_reduce(o_tok[:, (a["t"] + 1) % 2, :], o, o, 1.0, 0.0, ALU.mult, ALU.add,
                                                   stat[:, SS:SS + 1]).then_inc(sub_sum, 1)
                            dve.wait_ge(sub_sum, 8 * l + a["t"] + 1)
                            rstd(SR, SS, 1, 2 * HD)
                            STT(o, o, stat[:, SR:SR + 1], subg[:, l, :], ALU.mult, ALU.mult).then_inc(o_ready, 1)
                        else:
                            for half in range(2):
                                cols = slice(half * HD, (half + 1) * HD)
                                ins = TS(o[:, cols], ps[:, 6, cols], stat[:, RDEN + half:RDEN + half + 1], None, ALU.mult)
                                ins.then_inc(o_ready, 1) if half else step(ins)
                    elif kind == "turn_out":
                        _, i = tasks[a["t"]]
                        dve.wait_ge(ot_high, a["n"] + 1)
                        at_ = (slice(None), a["t"] // 2, slice(i * P, (i + 1) * P))
                        TT(ot_lo[at_], ps[:, 7, 0:P], ot_hi[at_].bitcast(F32), ALU.subtract).then_inc(misc_read, 1)
                    elif kind == "lift" and a["last"]:
                        dve.wait_ge(units_done, unit.split + 1)
                        for i in range(NT):
                            cols = slice(a["n"] * 512, (a["n"] + 1) * 512)
                            dve.wait_ge(bank_read[i], a["uses"][i])
                            if a["b"] == 0:
                                STT(merged[:, i, cols], tanh_g[:, i, :], 1.0, ps[:, i, :], ALU.add, ALU.mult)\
                                    .then_inc(bank_read[i], 1)
                                dve.wait_ge(bank_read[i], a["uses"][i] + 1)
                                V.memset(stat[:, 41:42], 0.0).then_inc(merged_done, 1)
                            else:
                                STT(lifted[:], tanh_g[:, i, :], 1.0, ps[:, i, :], ALU.add, ALU.mult)\
                                    .then_inc(bank_read[i], 1)
                                dve.wait_ge(bank_read[i], a["uses"][i] + 1)
                                TT(merged[:, i, cols], merged[:, i, cols], lifted[:], ALU.add).then_inc(merged_done, 1)
                                dve.wait_ge(merged_done, 12 * l + 4 * a["b"] + 2 * a["n"] + i + 1)
                    elif kind == "turn_merged":
                        turn_low(1 + 3 * l, 0.5)
                    elif kind == "out" and a["last"]:
                        dve.wait_ge(units_done, unit.split + 1)
                        dve.wait_ge(misc_read, plan.part_ready[l, 1])
                        for i in range(NT):
                            cols = slice(a["n"] * 512, (a["n"] + 1) * 512)
                            TT(lifted[:], ps[:, i, :], G1[:, cols], ALU.mult).then_inc(bank_read[i], 1)
                            dve.wait_ge(bank_read[i], a["uses"][i] + 1)
                            step(TT(x[:, i, cols], x[:, i, cols], lifted[:], ALU.add))

            def dense():
                def low(k, it=0):
                    slot, hl, _, s = dense_slots(k)
                    dve.wait_ge(high_done, it * 6 + s + 1)
                    TT(w_lo[:, hl, :], raw[:, slot, :], w_hi[:, hl, :].bitcast(F32), ALU.subtract).then_inc(low_done, 1)

                def block_(f, k, it=0, more=True):
                    b = f % 2
                    if more:
                        low(k, it)
                    dve.wait_ge(units_done, it * 6 + dense_split0 + dense_index(f, "up") + 1)
                    dve.wait_ge(d_silu, it * 2 + f + 1)
                    TT(act_t[:, b, :], silu_g[:, b, :], ps[:, 6 + b, 0:S], ALU.mult).then_inc(d_prod, 1)
                    if more:
                        low(k + 1, it)
                    dve.wait_ge(d_high, it * 2 + f + 1)
                    TT(act_lo[:, b, :], act_t[:, b, :], act_hi[:, b, :].bitcast(F32), ALU.subtract).then_inc(d_low, 1)
                    low(k + 2 if more else k, it)

                low(0)
                low(1)
                with dve.Fori(0, DENSE_LOOPS) as it:
                    block_(0, 2, it)
                    block_(1, 5, it)
                k = 2 + 6 * DENSE_LOOPS
                block_(FB - 2, k)
                block_(FB - 1, k + 3, more=False)
                dve.wait_ge(units_done, dense_split0 + 3 * FB)
                for i in range(NT):
                    for n in range(2):
                        cols = slice(n * 512, (n + 1) * 512)
                        step(TT(upd[:], ps[:, 2 * i + n, :], G2[:, cols], ALU.mult))
                        step(TT(x[:, i, cols], x[:, i, cols], upd[:], ALU.add))

            def routing():
                dve.wait_ge(router_mm, 1)
                dve.wait_ge(e_consts, 4)
                L = route[:, 5]
                step(V.tensor_copy(L, ps[:, 7, 0:NT * NE].rearrange("p (i e) -> p i e", i=NT)))
                for i in range(NT):
                    step(V.max(top_v[:, i, :], L[:, i, :]))
                    step(V.max_index(top_i[:, i, :], top_v[:, i, :], L[:, i, :]))
                step(V.tensor_copy(top_f[:], top_i[:]))
                TT(route[:, 0, :, 0:1], top_v[:, :, 1:2], top_v[:, :, 0:1], ALU.subtract).then_inc(route_exp_in, 1)
                dve.wait_ge(route_exp, 1)
                step(TS(route[:, 0, :, 2:3], route[:, 0, :, 1:2], 1.0, None, ALU.add))
                step(V.reciprocal(route[:, 0, :, 3:4], route[:, 0, :, 2:3]))
                step(TT(route[:, 0, :, 4:5], route[:, 0, :, 3:4], route[:, 0, :, 1:2], ALU.mult))
                for i in range(NT):
                    for j in range(2):
                        step(TS(route[:, 1 + j, i, :], iota_s[:, 0, 0:NE], top_f[:, i, j:j + 1], None, ALU.is_equal))
                    step(TS(route[:, 3, i, :], route[:, 1, i, :], route[:, 0, i, 3:4], None, ALU.mult))
                    step(STT(table[:, 2, i, 1:NE + 1], route[:, 2, i, :], route[:, 0, i, 4:5], route[:, 3, i, :],
                             ALU.mult, ALU.add))
                step(TT(table[:, 1, :, 1:NE + 1], route[:, 1], route[:, 2], ALU.add))
                V.tensor_copy(route[:, 4], table[:, 1, :, 1:NE + 1]).then_inc(member_done, 1)
                dve.wait_ge(rank_mm, 1)
                dve.wait_ge(member_done, 1)
                step(TT(table[:, 0, :, 1:NE + 1], ps[:, 7, 0:NT * NE].rearrange("p (i e) -> p i e", i=NT), route[:, 4],
                        ALU.subtract))
                step(V.tensor_reduce(flag_f[:], ps[:, 7, 2 * NE:3 * NE], AX_X, ALU.max))
                TS(flag[:], flag_f[:], float(P), None, ALU.is_gt).then_inc(flag_done, 1)

            def experts(n):
                e0 = n * NE

                def low(e, c, j):
                    k = j if isinstance(c, int) and c == 0 else j - 4
                    dve.wait_ge(e_high, (e + e0) * EU + round_unit(c, j) + 1)
                    TT(e_lo[:, k % HE, :], e_raw[:, k % RE, :], e_hi[:, k % HE, :].bitcast(F32), ALU.subtract)\
                        .then_inc(e_low, 1)

                def hidden_low(count):
                    dve.wait_ge(e_hhigh, count)
                    TT(he_lo[:], ps[:, 2, :].rearrange("p (k t) -> p k t", k=4), he_hi[:].bitcast(F32), ALU.subtract)\
                        .then_inc(e_hlow, 1)

                def gathered_low(count):
                    dve.wait_ge(e_xhigh, count)
                    V.tensor_copy(xg_lo[:, 0:4, :], ps[:, 7, :].rearrange("p (k t) -> p k t", k=4)).then_inc(e_xlow_a, 1)
                    V.tensor_copy(xg_lo[:, 4:8, :], ps[:, 0, :].rearrange("p (k t) -> p k t", k=4)).then_inc(e_xlow, 1)

                def pick_for(e):
                    for i in range(NT):
                        ins = TS(pick[:, i, :], iota_s[:, n, :], table[:, 0, i, bass.ds(e + 1, 1)],
                                 table[:, 1, i, bass.ds(e + 1, 1)], ALU.is_equal, ALU.mult)
                        if i == NT - 1:
                            ins.then_inc(e_pick, 1)
                        else:
                            ins.then_inc(e_pick_a, 1)

                def y_low(count):
                    dve.wait_ge(e_yhigh, count)
                    TT(y_lo[:], ps[:, 3:5, :].rearrange("p b n -> p (b n)"), y_hi[:].bitcast(F32), ALU.subtract)\
                        .then_inc(e_ylow, 1)

                def add_back(e, count):
                    for i in range(NT):
                        for h in range(2):
                            k = 2 * i + h
                            dve.wait_ge(e_back, (count - 1) * 4 + k + 1)
                            cols = slice(h * 512, (h + 1) * 512)
                            STT(moe[:, i, cols], ps[:, BACK[k], :], table[:, 2, i, bass.ds(e, 1)], moe[:, i, cols],
                                ALU.mult, ALU.add).then_inc(e_back_read, 1)

                def prod(count):
                    dve.wait_ge(e_silu, count)
                    TT(h_e[:], silu_e[:], ps[:, 1, :], ALU.mult).then_inc(e_prod, 1)

                def expert(e):
                    done = (e + e0) * EU
                    for j in range(5):
                        low(e, 0, j)
                    y_low((e + e0) + n + 1)
                    for j in range(5, 8):
                        low(e, 0, j)
                    add_back(e, (e + e0) + n + 1)
                    for j in range(LEAD):
                        low(e, 1, j)
                    dve.wait_ge(e_used, done + 8)
                    prod((e + e0) * NC + 1)
                    dve.wait_ge(e_pick_turned, (e + e0) + 1)
                    V.tensor_copy(pick_t[:], ps[:, 7, 0:NT * P].rearrange("p (i t) -> p i t", i=NT))
                    pick_for(e + 1)
                    with dve.Fori(1, NC) as c:
                        for j in range(LEAD, 9):
                            low(e, c, j)
                        hidden_low((e + e0) * NC + c)
                        for j in range(9, 12):
                            low(e, c, j)
                        dve.wait_ge(e_used, done + round_unit(c, 8))
                        prod((e + e0) * NC + c + 1)
                        for j in range(LEAD):
                            low(e, c + 1, j)
                    low(e, NC, 3)
                    hidden_low((e + e0) * NC + NC)
                    gathered_low((e + e0) + n + 2)

                V.memset(ps[:, 3:5, :], 0.0).then_inc(y_cleared, 1)
                pick_for(0)
                gathered_low(e0 + n + 1)
                expert(0)
                with dve.Fori(1, NE) as e:
                    expert(e)
                y_low(e0 + n + NE + 1)
                add_back(NE, e0 + n + NE + 1)
                dve.wait_ge(e_back_read, (NE + 1) * 4 * (n + 1))

            dve.wait_ge(consts_landed, 16 * N_LOADS)
            dve.wait_ge(bias_prod, 1)
            TT(vec[:], ps[0:N_BIAS + 1, 7, 0:NJ], block_sb[:], ALU.add).then_inc(misc_read, 1)
            for l in range(DEPTH):
                for k in range(2):
                    V.tensor_tensor_reduce(lam_junk[:], lamv[:, l, 2 * k, :], lamv[:, l, 2 * k + 1, :], 1.0, 0.0,
                                           ALU.mult, ALU.add, lam_s[:, l, k:k + 1]).then_inc(lam_sum, 1)
                    dve.wait_ge(lam_sum, 2 * l + k + 1)
                step(TS(subg[:, l, :], subg[:, l, :], 1.0 - lam_init(l), None, ALU.mult))
            dve.wait_ge(consts_split_hi, 2)
            TT(wf_lo[:], wf[:], wf_hi[:].bitcast(F32), ALU.subtract).then_inc(consts_split_lo, 1)
            TT(wr_lo[:], wr[:], wr_hi[:].bitcast(F32), ALU.subtract).then_inc(consts_split_lo, 1)
            dve.wait_ge(lam_exp, 1)
            for l in range(DEPTH):
                step(TT(neg_lam[:, l:l + 1], lam_s[:, l, 3:4], lam_s[:, l, 2:3], ALU.subtract))
                step(TS(neg_lam[:, l:l + 1], neg_lam[:, l:l + 1], -lam_init(l), None, ALU.add))
            dve.wait_ge(cs_ready, 1)
            first, ops = plan.segments["start"]
            for u in first:
                use(u)
            for kind, unit, a, ahead in ops:
                for u in ahead:
                    use(u)
                if kind == "mod_sum":
                    scale_part(a)
            dve.wait_ge(misc_read, plan.part_ready[0, 0])
            modulate(0, A1, SH1)
            turn_low(0)
            mixer(0)
            V.memset(stat[:, 42:43], 0.0).then_inc(x_ready, 1)
            dve.wait_ge(misc_read, plan.part_ready[0, 2])
            modulate(1, A2, SH2)
            turn_low(2)
            dense()
            V.memset(stat[:, 42:43], 0.0).then_inc(x_ready, 1)
            modulate(2, A1, SH1)
            turn_low(3)
            mixer(1)
            V.memset(stat[:, 42:43], 0.0).then_inc(x_ready, 1)
            modulate(3, A2, SH2)
            turn_low(5)
            dve.wait_ge(hh_done, 1)
            dve.wait_ge(h_ready, 8)
            TT(hl[:], htok[:], hh[:].bitcast(F32), ALU.subtract).then_inc(hl_done, 1)
            routing()
            experts(0)
            dve.wait_ge(flag_done, 1)
            more = dve.value_load(flag[0:1, 0:1], min_val=0, max_val=1)
            with dve.If(more > 0):
                experts(1)
            for i in range(NT):
                step(TT(moe[:, i, :], moe[:, i, :], G2, ALU.mult))
                ins = TT(x[:, i, :], x[:, i, :], moe[:, i, :], ALU.add)
                ins.then_inc(h_final, 1) if i == NT - 1 else step(ins)
            dve.wait_ge(final_sq, 2)
            rstd(RS, SQ, NT, D)
            dve.wait_ge(gain_landed, 16 * 5)
            for i in range(NT):
                ins = STT(x[:, i, :], x[:, i, :], stat[:, RS + i:RS + i + 1], gain[:], ALU.mult, ALU.mult)
                ins.then_inc(out_ready, 1) if i == NT - 1 else step(ins)


_INS = ["x", "c", "norm_mix_g", "norm_ffn_g", "w_mod", "b_mod", "w_in", "b_forget", "lam_q1", "lam_k1", "lam_q2",
        "lam_k2", "subln_g", "rel_bias", "w_br_a", "w_br_b", "w_br_c", "w_out", "w_ff_gate", "w_ff_up",
        "w_ff_down", "w_router", "w_exp_gate", "w_exp_up", "w_exp_down", "final_norm_g"]


def kernel(**inputs):
    import concourse.bacc as bacc
    from concourse.bass_utils import run_bass_kernel_spmd

    nc = bacc.Bacc("TRN2", target_bir_lowering=False, num_devices=1)
    arrays = {f"in_{name}": np.ascontiguousarray(inputs[name]) for name in _INS}
    arrays["in_buckets"], arrays["in_blocked"] = shape_tables()
    args = [nc.dram_tensor(name, a.shape, mybir.dt.from_np(a.dtype), kind="ExternalInput").ap()
            for name, a in arrays.items()]
    out = nc.dram_tensor("out_0", (1, S, D), F32, kind="ExternalOutput").ap()
    trunk(nc, *args, out)
    r = run_bass_kernel_spmd(nc, [arrays], core_ids=[0])
    return r.results[0]["out_0"]
```

```python
import math
from contextlib import ExitStack

import concourse.bass as bass
import numpy as np
from concourse import mybir

F32 = mybir.dt.float32
F32R = mybir.dt.float32r
I32 = mybir.dt.int32
U32 = mybir.dt.uint32
ALU = mybir.AluOpType
ACT = mybir.ActivationFunctionType
AX_X = mybir.AxisListType.X

P = 128
S = 256
NT = S // P
D = 1024
KB = D // P
DEPTH = 2
HD = 64
A_HEADS, B_HEADS, C_HEADS, GROUPS = 4, 6, 6, ((128, 1), (512, 4), (2048, 16))
G = len(GROUPS)
A_W, B_W, C_W = A_HEADS * 2 * HD, B_HEADS * HD, C_HEADS * HD
QA, KA, VA = 0, A_W, 2 * A_W
QB = 3 * A_W
KBC, VB = QB + G * B_W, QB + 2 * G * B_W
QC = QB + 3 * G * B_W
KC, VC = QC + C_W, QC + 2 * C_W
FC = QC + 3 * C_W
GC = FC + C_HEADS
N_IN = GC + 3 * D
N_BUCKETS, REL_MAX_DIST = 32, 2048
N_BIAS = 2 * A_HEADS + G * B_HEADS
D_FF = 2816
NE, FE = 8, 3584
EPS = 1e-6
VW = A_W + G * B_W + C_W
OW = (A_W + B_W + C_W) // P
FLIPS = -(-(N_BIAS + 1) // 2)
BLOCKED = -1e30
NJ = 384
CH = 512
NC = FE // CH

UM = 1024
R, H = 6, 3
RE, HE = 12, 6


def lam_init(l):
    return 0.8 - 0.6 * math.exp(-0.3 * l)


def shape_tables():
    dist = S - 1 - np.arange(NJ)
    n = np.maximum(dist, 0)
    exact = N_BUCKETS // 2
    nf = np.maximum(n, 1).astype(np.float32)
    large = exact + (np.log(nf / np.float32(exact)) / np.float32(math.log(REL_MAX_DIST / exact))
                     * np.float32(N_BUCKETS - exact)).astype(np.int32)
    bucket = np.where(n < exact, n, np.minimum(large, N_BUCKETS - 1))
    onehot = (np.arange(N_BUCKETS)[:, None] == bucket[None]).astype(np.float32)
    sees = np.tile(dist >= 0, (N_BIAS + 1, 1))
    for g, (window, dil) in enumerate(GROUPS):
        r = slice(2 * A_HEADS + g * B_HEADS, 2 * A_HEADS + (g + 1) * B_HEADS)
        sees[r] &= ((dist % dil == 0) & (dist <= window))[None]
    return onehot, np.where(sees, 0.0, BLOCKED).astype(np.float32)


class Unit:

    def __init__(self, src, shape, mod=None):
        self.src, self.shape, self.mod = src, shape, mod


def mixer_ops(l, w):
    w_in = w["w_in"][l].rearrange("(kb p) n -> p kb n", p=P)
    w_br = [w[n][l].rearrange("(kb p) n -> p kb n", p=P) for n in ("w_br_a", "w_br_b", "w_br_c")]
    w_out = w["w_out"][l].rearrange("(kb p) n -> p kb n", p=P)

    def qk(pair):
        if pair < 4:
            cols = [QA + P * pair, KA + P * pair]
        elif pair < 7:
            cols = [base + g * B_W + P * (pair - 4) for base in (QB, KBC) for g in range(G)]
        else:
            cols = [QC + P * (pair - 7), KC + P * (pair - 7)]
        half = len(cols) // 2
        return [("qk", Unit(w_in[:, :, c:c + P], (KB, P)), dict(pair=pair, j=(j % half) + 3 * (j // half)))
                for j, c in enumerate(cols)]

    def wide(kind, view, kbs, c0, width, **args):
        ops = []
        for k0 in range(0, kbs, 2):
            nk = min(2, kbs - k0)
            ops.append((kind, Unit(view[:, k0:k0 + nk, c0:c0 + width], (nk, width)),
                        dict(k0=k0, first=k0 == 0, last=k0 + nk == kbs, width=width, **args)))
        return ops

    va = wide("v", w_in, KB, VA, A_W, dst=0)
    vb = [o for c in range(0, G * B_W, 512)
          for o in wide("v", w_in, KB, VB + c, min(512, G * B_W - c), dst=A_W + c)]
    vc = wide("v", w_in, KB, VC, C_W, dst=A_W + G * B_W)

    def merge(b, n):
        gate = wide("gate", w_in, KB, GC + b * D + n * 512, 512, b=b, n=n)
        lift = wide("lift", w_br[b], (4, 3, 3)[b], n * 512, 512, b=b, n=n)
        return gate + lift

    fills = [[] for _ in range(20)]
    for t, f in ((0, qk(1) + vb[:5]), (2, vb[5:8] + qk(2) + vb[8:10]), (4, vb[10:] + qk(3) + vc[:3]),
                 (6, vc[3:] + qk(4)), (8, qk(5)), (10, qk(6) + merge(0, 0)[:1]), (12, merge(0, 0)[1:] + qk(7)),
                 (14, qk(8) + merge(0, 1)), (16, qk(9) + merge(1, 0)), (18, merge(1, 1))):
        fills[t], fills[t + 1] = f[:len(f) // 2], f[len(f) // 2:]
    ops = [("forget", None, {})] + qk(0)[:1] + [("forget_turn", None, {})] + qk(0)[1:] + va + [("cumsum", None, {})]
    if l == 0:
        ops = ops[:2] + [o for i, u in enumerate(ops[2:]) for o in [u] + [("flip", None, dict(n=n)) for n in
               range(i * FLIPS // len(ops[2:]), (i + 1) * FLIPS // len(ops[2:]))]]
    for t in range(20):
        f = fills[t]
        cut = max(1, len(f) - 1 - (len(f) > 3))
        if t > 1:
            ops += [("turn_out", None, dict(t=t - 2))]
        ops += [("scores", None, dict(t=t))]
        ops += [("weigh", None, dict(t=t))]
        if t:
            ops += [("finish", None, dict(t=t - 1))]
        ops += f[:cut] + [("turn_probs", None, dict(t=t))]
        if t:
            ops += [("norm_out", None, dict(t=t - 1))]
        ops += f[cut:] + [("values", None, dict(t=t))]
    final = merge(2, 0) + merge(2, 1)
    ops += [("turn_out", None, dict(t=18))] + final[:1]
    ops += [("finish", None, dict(t=19)), ("turn_out", None, dict(t=19))] + final[1:]
    ops += [("turn_merged", None, {})]
    for n in range(2):
        ops += wide("out", w_out, KB, n * 512, 512, n=n)

    mods = [(l, 1), (l, 2)] + [(l + 1, 0)] * (l + 1 < DEPTH)
    todo = [o for (ml, part) in mods for o in mod_ops(ml, part, w)]
    woven, done = [("gain", None, dict(src="norm_ffn_g", l=l))], 0
    if l + 1 < DEPTH:
        todo.insert(len(todo) - 8, ("gain", None, dict(src="norm_mix_g", l=l + 1)))
    last = max(i for i, o in enumerate(ops) if o[0] == "turn_merged") - 8
    spare = [{"qk": 0, "v": 3, "gate": 3, "lift": 3, "scores": 2, "values": 2}.get(o[0], 0) for o in ops[:last]]
    for i, o in enumerate(ops):
        woven.append(o)
        if i < last:
            upto = len(todo) * sum(spare[:i + 1]) // sum(spare)
            woven += todo[done:upto]
            done = upto
    assert done == len(todo)
    if l + 1 == DEPTH:
        woven.append(("gain", None, dict(src="final_norm_g", l=0)))
    return woven


def mod_ops(l, part, w):
    view = w["w_mod"][l].rearrange("(kb p) n -> p kb n", p=P)
    ops = []
    for kb in range(KB):
        for half in range(2):
            c0 = part * 2048 + half * UM
            ops.append(("mod", Unit(view[:, kb:kb + 1, c0:c0 + UM], (1, UM), mod=(l, part, kb, half)), {}))
    return ops + [("mod_sum", None, dict(l=l, part=part, n=n)) for n in range(4)]


class Plan:

    def __init__(self, w):
        self.raw_n = self.split_n = self.mod_n = 0
        self.owner = [None] * R
        self.segments = {}
        self.units = {}
        self.bank = [0, 0]
        self.turned = self.upper = 0
        self.sums = 0
        self.groups = 0
        self.gain_used = None
        self.qk_ready, self.v_ready = {}, {}
        self.qk_turn = 0
        self.misc = 1
        self.outs_ready = {}
        self.part_ready = {}
        self.tasks = self.scores = 0
        start = mod_ops(0, 0, w)
        self.segment("start", start[:8] + [("gain", None, dict(src="norm_mix_g", l=0))] + start[8:12] +
                     [("x", None, {})] + start[12:])
        self.segment("mix0", mixer_ops(0, w))

    def unit(self, u):
        u.raw = self.raw_n % R
        u.landed = 16 * (self.raw_n // R + 1)
        u.waits = self.owner[u.raw]
        if u.mod is None:
            u.split = self.split_n
            u.hl = self.split_n % H
            self.split_n += 1
            self.owner[u.raw] = ("split", u.split)
        else:
            u.nth = self.mod_n
            self.mod_n += 1
            self.owner[u.raw] = ("mod", u.nth)
        self.raw_n += 1

    def segment(self, name, ops):
        out = []
        for kind, unit, a in ops:
            a = dict(a)
            if unit is not None:
                self.unit(unit)
            if kind == "qk":
                b = self.qk_turn % 2
                self.qk_turn += 1
                a.update(bank=b, uses=self.bank[b])
                self.bank[b] += 1
                self.qk_ready[a["pair"]] = tuple(self.bank)
            elif kind in ("v", "gate", "lift", "out"):
                a["uses"] = tuple(self.bank)
                if a["last"]:
                    self.groups += 1
                    a["group"] = self.groups
                    self.bank = [self.bank[0] + 1, self.bank[1] + 1]
                    if kind == "v":
                        self.v_ready[sum(a["dst"] >= e for e in (A_W, A_W + G * B_W))] = tuple(self.bank)
            elif kind in ("turn_out", "cumsum", "mod_sum", "forget", "forget_turn"):
                a["misc"] = self.misc
                a["odd_bank"] = 2 + a["n"] if name == "start" else 7
                self.misc += 1
                if kind == "mod_sum":
                    a["nth"] = self.sums
                    self.sums += 1
                    self.part_ready[a["l"], a["part"]] = self.misc
                    if not plain_part(a["part"], a["n"]):
                        self.gain_used = self.misc
            elif kind == "scores":
                pair = a["t"] // 2
                a.update(n=self.tasks, ready=self.qk_ready[pair], turned=self.turned, upper=self.upper)
                self.tasks += 1
            elif kind == "turn_probs":
                a.update(n=self.tasks - 1, turned=self.turned, upper=self.upper)
                two = a["t"] >= 8
                self.turned += 1 + two
                self.upper += two
            elif kind == "values":
                branch = (a["t"] >= 8) + (a["t"] >= 14)
                a.update(n=self.tasks - 1, ready=self.v_ready[branch], upper=self.upper)
            elif kind == "gain":
                a["used"] = self.gain_used
            if kind == "turn_out":
                if a["t"] in (7, 13, 19):
                    self.outs_ready[(7, 13, 19).index(a["t"])] = self.misc
            if kind == "lift":
                a["outs"] = self.outs_ready[a["b"]]
            if kind == "scores":
                a["cumsum"] = self.cumsum
            if kind == "cumsum":
                self.cumsum = self.misc
            if kind == "weigh":
                a["n"] = self.tasks - 1
            if kind in ("finish", "turn_out"):
                a["n"] = (self.tasks - 1) // 20 * 20 + a["t"]
            out.append((kind, unit, a))
        units = [u for _, u, _ in out if u is not None]
        ahead, at, splits = [], 0, 0
        for kind, unit, _ in [(None, None, None)] + out:
            splits += unit is not None and unit.mod is None
            now = []
            while at < len(units):
                u = units[at]
                ahead_of = u.mod is None and units_split(units, at) > splits + 1
                if ahead_of:
                    break
                now.append(u)
                at += 1
            ahead.append(now)
        self.segments[name] = (ahead[0], [(*o, ahead[i + 1]) for i, o in enumerate(out)])
        self.units[name] = units
        return out


def plain_part(part, n):
    return not (part == 0 and n >= 2 or part == 2 and n < 2)


def units_split(units, at):
    return sum(u.mod is None for u in units[:at])


def trunk(nc, x_in, c, norm_mix_g, norm_ffn_g, w_mod, b_mod, w_in, b_forget, lam_q1, lam_k1, lam_q2, lam_k2,
          subln_g, rel_bias, w_br_a, w_br_b, w_br_c, w_out, w_ff_gate, w_ff_up, w_ff_down, w_router,
          w_exp_gate, w_exp_up, w_exp_down, final_norm_g, buckets, blocked, out):
    w = dict(w_mod=w_mod, w_in=w_in, w_br_a=w_br_a, w_br_b=w_br_b, w_br_c=w_br_c, w_out=w_out)
    plan = Plan(w)
    FB = D_FF // P
    wg = w_ff_gate[0].rearrange("(kb p) n -> p kb n", p=P)
    wu = w_ff_up[0].rearrange("(kb p) n -> p kb n", p=P)
    wd = w_ff_down[0].rearrange("(fb p) n -> p fb n", p=P)
    DENSE_LOOPS = (FB - 2) // 2
    dense_raw0, dense_split0 = plan.raw_n, plan.split_n
    assert all(o == ("split", dense_split0 - R + (k - dense_raw0) % R) for k, o in
               ((k, plan.owner[k % R]) for k in range(dense_raw0, dense_raw0 + R)))
    plan.raw_n += 3 * FB
    plan.split_n += 3 * FB
    for k in range(plan.raw_n - R, plan.raw_n):
        plan.owner[k % R] = ("split", plan.split_n - plan.raw_n + k)
    plan.segment("mix1", mixer_ops(1, w))
    gains = dict(norm_mix_g=norm_mix_g, norm_ffn_g=norm_ffn_g, final_norm_g=final_norm_g)

    with ExitStack() as ctx:
        at = [nc.sbuf_base // 32 * 32 + 32]

        def place(name, shape, dt=F32, where=None):
            size = 4 * int(np.prod(shape[1:]))
            size = (size + 31) // 32 * 32
            offset = at[0] if where is None else where
            t = nc.alloc_sbuf_tensor_at(name, shape, dt, offset=offset)
            assert offset + size <= nc.sbuf_usable_end, (name, offset, size)
            if where is None:
                at[0] += size
            return t

        x = place("x", [P, NT, D])
        mod = place("mod", [P, 3, 2 * D])
        gain = place("gain", [P, D])
        ident = place("ident", [P, P])
        ident_r = place("ident_r", [P, P], F32R)
        ones = place("ones", [P, P])
        anti = place("anti", [P, P])
        neg_ident = place("neg_ident", [P, 8])
        tri = place("tri", [P, NT, S])
        cond = place("cond", [P, KB])
        cs = place("cs", [P, KB])
        lam_s = place("lam_s", [P, DEPTH, 4])
        neg_lam = place("neg_lam", [P, DEPTH])
        subg = place("subg", [P, DEPTH, 2 * HD])
        bf = place("bf", [P, DEPTH, C_HEADS])
        wf = place("wf", [P, DEPTH, KB, C_HEADS])
        wf_hi = place("wf_hi", [P, DEPTH, KB, C_HEADS], F32R)
        wf_lo = place("wf_lo", [P, DEPTH, KB, C_HEADS], F32R)
        wr = place("wr", [P, KB, NE])
        wr_hi = place("wr_hi", [P, KB, NE], F32R)
        wr_lo = place("wr_lo", [P, KB, NE], F32R)
        stat = place("stat", [P, 64])
        lf = place("lf", [P, NT, C_HEADS])
        lf_t = place("lf_t", [P, 3, NT, C_HEADS])
        ft = place("ft", [NE, S])
        ht_at = at[0]
        ht_hi = place("ht_hi", [P, KB, S], F32R)
        ht_lo = place("ht_lo", [P, KB, S], F32R)
        merged = place("merged", [P, NT, D])
        htok = merged
        zero_r = place("zero_r", [P, P], F32R)
        arena = at[0]
        raw = place("raw", [P, R, UM])
        w_hi = place("w_hi", [P, H, UM], F32R)
        w_lo = place("w_lo", [P, H, UM], F32R)
        arena2 = at[0]
        bias = place("bias", [P, N_BIAS + 1, S])
        qkt = place("qkt", [P, 2, 6, S])
        vals = place("vals", [P, NT, VW])
        arena3 = at[0]
        prob = place("prob", [P, 2, 3 * S])
        prob_t = place("prob_t", [P, 2, 3 * S])
        o_tok = place("o_tok", [P, 2, P])
        ot_hi = place("ot_hi", [P, OW, S], F32R)
        ot_lo = place("ot_lo", [P, OW, S], F32R)
        tanh_g = place("tanh_g", [P, NT, 512], where=arena2)
        lifted = place("lifted", [P, 512], where=arena2 + 4 * NT * 512)
        rel = place("rel", [N_BUCKETS, N_BIAS + 1], where=arena3)
        buck = place("buck", [N_BUCKETS, NJ], where=arena3 + 128)
        block_sb = place("block_sb", [N_BIAS + 1, NJ], where=arena3 + 128 + 4 * NJ)
        vec = place("vec", [N_BIAS + 1, NJ], where=arena3 + 128 + 8 * NJ)
        lamv = place("lamv", [P, DEPTH, 4, HD], where=arena3 + 128 + 12 * NJ)
        lam_junk = place("lam_junk", [P, HD], where=arena3 + 128 + 12 * NJ + 32 * HD)
        silu_g = place("silu_g", [P, 2, S], where=arena3)
        act_t = place("act_t", [P, 2, S], where=arena3 + 8 * S)
        act_hi = place("act_hi", [P, 2, S], F32R, where=arena3 + 16 * S)
        act_lo = place("act_lo", [P, 2, S], F32R, where=arena3 + 24 * S)
        upd = place("upd", [P, 512], where=arena3 + 32 * S)
        e_hi = place("e_hi", [P, HE, UM], F32R, where=arena)
        e_lo = place("e_lo", [P, HE, UM], F32R, where=arena + 4 * HE * UM)
        assert arena + 8 * HE * UM <= arena2
        e_raw = place("e_raw", [P, RE, UM], where=arena3 - 4 * RE * UM)
        assert arena3 - 4 * RE * UM >= arena2 + 4 * (NT + 1) * 512
        e_at = [arena3]

        def eplace(name, shape, dt=F32):
            t = place(name, shape, dt, where=e_at[0])
            e_at[0] += (4 * int(np.prod(shape[1:])) + 31) // 32 * 32
            return t

        hh = eplace("hh", [P, NT, D], F32R)
        hl = eplace("hl", [P, NT, D], F32R)
        y_hi = eplace("y_hi", [P, D], F32R)
        y_lo = eplace("y_lo", [P, D], F32R)
        moe = merged
        xg_hi = place("xg_hi", [P, KB, P], F32R, where=ht_at)
        xg_lo = place("xg_lo", [P, KB, P], F32R, where=ht_at + 4 * KB * P)
        h_e = place("h_e", [P, CH], where=ht_at + 8 * KB * P)
        silu_e = place("silu_e", [P, CH], where=ht_at + 8 * KB * P + 4 * CH)
        he_hi = place("he_hi", [P, 4, P], F32R, where=ht_at + 8 * KB * P + 8 * CH)
        he_lo = place("he_lo", [P, 4, P], F32R, where=ht_at + 8 * KB * P + 12 * CH)
        pick = eplace("pick", [P, NT, P], F32R)
        pick_t = eplace("pick_t", [P, NT, P], F32R)
        iota_s = eplace("iota_s", [P, 2, P])
        route = eplace("route", [P, 8, NT, NE])
        top_v = eplace("top_v", [P, NT, 8])
        top_i = eplace("top_i", [P, NT, 8], U32)
        top_f = eplace("top_f", [P, NT, 8])
        table = eplace("table", [P, 3, NT, NE + 2])
        counts = eplace("counts", [P, NE])
        flag = eplace("flag", [P, 1], I32)
        flag_f = eplace("flag_f", [P, 1])
        assert e_at[0] <= nc.sbuf_usable_end

        ps = ctx.enter_context(nc.psum_tensor("ps", [P, 8, 512], F32))
        scratch = nc.dram_tensor("bias_rows", [N_BIAS + 1, NJ], F32, kind="Internal").ap()
        kept = nc.dram_tensor("bias_of_a", [P, 2 * A_HEADS, S], F32, kind="Internal").ap()
        bias_flat = bias[:].rearrange("p m k -> p (m k)")

        def sem(name):
            return ctx.enter_context(nc.semaphore(name))

        consts_landed = sem("consts_landed")
        consts_made = sem("consts_made")
        rel_cleared = sem("rel_cleared")
        ident_r_made = sem("ident_r_made")
        consts_split_hi = sem("consts_split_hi")
        consts_split_lo = sem("consts_split_lo")
        bias_prod = sem("bias_prod")
        bias_rows = sem("bias_rows")
        bias_landed = sem("bias_landed")
        flip_mm = sem("flip_mm")
        flip_read = sem("flip_read")
        bias_kept = sem("bias_kept")
        bias_back = sem("bias_back")
        x_landed = sem("x_landed")
        cond_landed = sem("cond_landed")
        cs_ready = sem("cs_ready")
        lam_sum = sem("lam_sum")
        lam_exp = sem("lam_exp")
        gain_landed = sem("gain_landed")
        high_done = sem("high_done")
        low_done = sem("low_done")
        units_done = sem("units_done")
        tile0_done = sem("tile0_done")
        mod_used = sem("mod_used")
        mod_zero = sem("mod_zero")
        part0_cleared = sem("part0_cleared")
        mod_mm = sem("mod_mm")
        misc_read = sem("misc_read")
        sq_done = sem("sq_done")
        h_ready = sem("h_ready")
        h_final = sem("h_final")
        merged_done = sem("merged_done")
        turned = sem("turned")
        ht_high = sem("ht_high")
        ht_low = sem("ht_low")
        forget_raw = sem("forget_raw")
        forget_mm = sem("forget_mm")
        forget_pre = sem("forget_pre")
        forget_exp = sem("forget_exp")
        forget_ln = sem("forget_ln")
        forget_log = sem("forget_log")
        cum_mm = sem("cum_mm")
        scores_done = sem("scores_done")
        biased = sem("biased")
        exp_done = sem("exp_done")
        diff_done = sem("diff_done")
        probs_turned = sem("probs_turned")
        pt_low = sem("pt_low")
        pt_up = sem("pt_up")
        values_done = sem("values_done")
        o_taken = sem("o_taken")
        o_normed = sem("o_normed")
        sub_sum = sem("sub_sum")
        sub_rstd = sem("sub_rstd")
        pool_step = sem("pool_step")
        out_turned = sem("out_turned")
        ot_high = sem("ot_high")
        x_ready = sem("x_ready")
        d_silu = sem("d_silu")
        d_tile0 = sem("d_tile0")
        d_prod = sem("d_prod")
        d_high = sem("d_high")
        d_low = sem("d_low")
        router_raw = sem("router_raw")
        router_copied = sem("router_copied")
        router_mm = sem("router_mm")
        route_exp_in = sem("route_exp_in")
        route_exp = sem("route_exp")
        member_done = sem("member_done")
        rank_mm = sem("rank_mm")
        flag_done = sem("flag_done")
        hh_done = sem("hh_done")
        hl_done = sem("hl_done")
        e_consts = sem("e_consts")
        e_high = sem("e_high")
        e_low = sem("e_low")
        e_used = sem("e_used")
        e_silu = sem("e_silu")
        e_prod = sem("e_prod")
        e_turned = sem("e_turned")
        e_hhigh = sem("e_hhigh")
        e_hlow = sem("e_hlow")
        e_pick = sem("e_pick")
        e_gather = sem("e_gather")
        e_xhigh = sem("e_xhigh")
        e_xlow = sem("e_xlow")
        e_yhigh = sem("e_yhigh")
        e_ylow = sem("e_ylow")
        e_back = sem("e_back")
        e_back_read = sem("e_back_read")
        e_pick_turned = sem("e_pick_turned")
        y_cleared = sem("y_cleared")
        store_done = sem("store_done")
        out_ready = sem("out_ready")
        final_sq = sem("final_sq")
        dve_step = sem("dve_step")
        raw_landed = [sem(f"raw_landed{i}") for i in range(R)]
        e_landed = [sem(f"e_landed{i}") for i in range(RE)]
        mod_start = [[sem(f"mod_start{l}{part}") for part in range(3)] for l in range(DEPTH)]
        bank_read = [sem("bank0_read"), sem("bank1_read")]

        block = ctx.enter_context(nc.Block())
        tasks = [(p, i) for p in range(10) for i in range(NT)]
        def flat_scores(half):
            return ps[:, 2 + 2 * half:4 + 2 * half, :].rearrange("p b n -> p (b n)")

        def dense_index(f, what):
            return {"gate": 3 * f - (f > 0), "up": 3 * f + (f == 0), "down": 3 * f + 4 - 2 * (f == FB - 1)}[what]

        N_LOADS = 10 + 4 * DEPTH
        EU = 12 * NC
        LEAD = 3
        SQ, RS, DEN, NMAX, SS, SR, COEF, RDENS = 0, 2, 4, 6, 8, 10, 14, (12, 24)
        SH1, A1, G1, SH2, A2, G2 = [mod[:, k // 2, (k % 2) * D:(k % 2 + 1) * D] for k in range(6)]

        def maps(pair):
            return 3 if 4 <= pair < 7 else 1

        def bias_of(pair, half):
            if pair < 4:
                return 2 * pair + half
            if pair < 7:
                return 2 * A_HEADS + 3 * (2 * (pair - 4) + half)
            return N_BIAS

        def rstd(E, step, dst, src, tmp, width, size):
            y, s_ = stat[:, dst:dst + width], stat[:, src:src + width]
            a_, t = stat[:, tmp:tmp + width], stat[:, tmp + 2:tmp + 2 + width]
            step(E.tensor_scalar(a_, s_, 1.0 / size, EPS, ALU.mult, ALU.add))
            step(E.tensor_scalar(y.bitcast(I32), a_.bitcast(I32), -0.5, float(0x5F3759DF), ALU.mult, ALU.add))
            step(E.tensor_scalar(a_, a_, -0.5, None, ALU.mult))
            for _ in range(3):
                if width == 1:
                    step(E.tensor_scalar(t, y, y, a_, ALU.mult, ALU.mult))
                    step(E.tensor_scalar(y, t, 1.5, y, ALU.add, ALU.mult))
                else:
                    step(E.tensor_tensor(t, y, y, ALU.mult))
                    step(E.tensor_tensor(t, t, a_, ALU.mult))
                    step(E.scalar_tensor_tensor(y, t, 1.5, y, ALU.add, ALU.mult))

        def tile_done(engine, i, unit, a):
            if i == 0:
                engine.wait_ge(tile0_done, a["group"])
            else:
                engine.wait_ge(units_done, unit.split + 1)

        def unit_view(ring, slot, u):
            n, width = u.shape
            return ring[:, slot, 0:n * width].rearrange("p (k n) -> p k n", k=n)

        def by_map(buf, n, i):
            return buf[:, 0:n * S].rearrange("p (m k) -> p m k", m=n)[:, :, 0:(i + 1) * P]

        def dense_slots(k):
            r, s = dense_raw0 + k, dense_split0 + k
            return r % R, s % H, r // R, s

        def expert_src(e, c, j):
            one = bass.ds(e, 1)
            if j < 8:
                view = (w_exp_gate, w_exp_up)[j // 4][0].rearrange("e (kb p) n -> e p kb n", p=P)
                src = view[one, :, 2 * (j % 4):2 * (j % 4) + 2, bass.ds(c * CH, CH)]
            else:
                view = w_exp_down[0].rearrange("e (fb p) n -> e p fb n", p=P)
                src = view[one, :, bass.ds((c - 1) * 4 + j - 8, 1), :]
            return src.rearrange("a p k n -> p (a k) n")

        BACK = (5, 6, 7, 2)

        def round_unit(c, j):
            return c * 12 + (j if isinstance(c, int) and c == 0 else j - 4)

        @block.sync
        def _(sp):
            def load_segment(name):
                for kind, u, a, _ in plan.segments[name][1]:
                    if kind == "x":
                        sp.dma_start(x[:], x_in[0].rearrange("(i p) d -> p i d", p=P)).then_inc(x_landed, 16)
                    elif kind == "gain":
                        if a["used"] is not None:
                            sp.wait_ge(misc_read, a["used"])
                        src = gains[a["src"]]
                        src = src[a["l"]] if a["src"] != "final_norm_g" else src
                        sp.dma_start(gain[:], src.partition_broadcast(P)).then_inc(gain_landed, 16)
                    elif u is not None:
                        if u.waits is not None:
                            sp.wait_ge(low_done if u.waits[0] == "split" else mod_used, u.waits[1] + 1)
                        sp.dma_start(unit_view(raw, u.raw, u), u.src).then_inc(raw_landed[u.raw], 16)

            def dense(k, src, nk, it=0):
                slot, _, _, s = dense_slots(k)
                sp.wait_ge(low_done, it * 6 + s - R + 1)
                sp.dma_start(raw[:, slot, :].rearrange("p (k n) -> p k n", k=nk), src)\
                    .then_inc(raw_landed[slot], 16)

            sp.wait_ge(part0_cleared, 1)
            sp.dma_start(mod[0:1, 0, :], b_mod[0:1, 0:2 * D]).then_inc(mod_start[0][0], 16)
            load_segment("start")
            load_segment("mix0")
            dense(0, wg[:, :, 0:P], KB)
            dense(1, wu[:, :, 0:P], KB)
            with sp.Fori(0, DENSE_LOOPS) as it:
                for f in range(2):
                    dense(2 + 3 * f, wg[:, :, bass.ds((it * 2 + 1 + f) * P, P)], KB, it)
                    dense(3 + 3 * f, wu[:, :, bass.ds((it * 2 + 1 + f) * P, P)], KB, it)
                    dense(4 + 3 * f, wd[:, bass.ds(it * 2 + f, 1), :], 1, it)
            k = 2 + 6 * DENSE_LOOPS
            dense(k, wg[:, :, (FB - 1) * P:FB * P], KB)
            dense(k + 1, wu[:, :, (FB - 1) * P:FB * P], KB)
            dense(k + 2, wd[:, FB - 2:FB - 1, :], 1)
            dense(k + 3, wd[:, FB - 1:FB, :], 1)
            load_segment("mix1")

            sp.wait_ge(values_done, len(tasks) * DEPTH)

            def expert_unit(e, c, j, base, kind=None):
                kind = j if kind is None else kind
                slot = (j if isinstance(c, int) and c == 0 else j - 4) % RE
                k = e * EU + round_unit(c, j) + base
                if not isinstance(k, int) or k >= RE:
                    sp.wait_ge(e_low, k - RE + 1)
                sp.dma_start(e_raw[:, slot, :].rearrange("p (k n) -> p k n", k=2 if kind < 8 else 1),
                             expert_src(e, c, kind)).then_inc(e_landed[slot], 16)

            def expert(e, base):
                first = isinstance(e, int) and base == 0
                for j in range(8):
                    expert_unit(e, 0, j, base)
                if first:
                    for j in range(12):
                        expert_unit(e, 1, j, base)
                with sp.Fori(1 + first, NC) as c:
                    for j in range(12):
                        expert_unit(e, c, j, base)
                for j in range(4):
                    expert_unit(e, NC, j, base, kind=8 + j)

            expert(0, 0)
            with sp.Fori(1, NE) as e:
                expert(e, 0)
            sp.wait_ge(flag_done, 1)
            more = sp.value_load(flag[0:1, 0:1], min_val=0, max_val=1)
            with sp.If(more > 0):
                with sp.Fori(0, NE) as e:
                    expert(e, NE * EU)
            for i in range(NT):
                sp.wait_ge(out_ready, i + 1)
                sp.dma_start(out[0, i * P:(i + 1) * P, :], x[:, i, :]).then_inc(store_done, 16)
            sp.wait_ge(store_done, 16 * NT)

        @block.gpsimd
        def _(pool):
            g = nc.gpsimd
            g.memset(rel[:], 0.0).then_inc(rel_cleared, 1)
            def mod_begin(l, part, n):
                g.memset(mod[:, part, :], 0.0).then_inc(mod_zero, 1)
                pool.wait_ge(mod_zero, n + 1)
                pool.dma_start(mod[0:1, part, :], b_mod[l:l + 1, part * 2 * D:(part + 1) * 2 * D])\
                    .then_inc(mod_start[l][part], 16)

            g.memset(ones[:], 1.0).then_inc(consts_made, 1)
            g.memset(ident[:], 0.0).then_inc(consts_made, 1)
            g.memset(neg_ident[:], 0.0).then_inc(consts_made, 1)
            g.memset(tri[:], 1.0).then_inc(consts_made, 1)
            g.memset(zero_r[:].bitcast(F32), 0.0).then_inc(consts_made, 1)
            g.memset(anti[:], 0.0).then_inc(consts_made, 1)
            pool.wait_ge(consts_made, 6)
            g.affine_select(out=anti[:], in_=anti[:], compare_op=ALU.not_equal, fill=1.0, base=-(P - 1),
                            pattern=[[1, P]], channel_multiplier=1).then_inc(consts_made, 1)
            g.affine_select(out=ident[:], in_=ident[:], compare_op=ALU.not_equal, fill=1.0, base=0,
                            pattern=[[-1, P]], channel_multiplier=1).then_inc(consts_made, 1)
            g.affine_select(out=neg_ident[:], in_=neg_ident[:], compare_op=ALU.not_equal, fill=-1.0, base=0,
                            pattern=[[-1, 8]], channel_multiplier=1).then_inc(consts_made, 1)
            g.affine_select(out=tri[:], in_=tri[:], compare_op=ALU.is_ge, fill=0.0, base=0,
                            pattern=[[-P, NT], [1, S]], channel_multiplier=-1).then_inc(consts_made, 1)
            mod_begin(0, 1, 0)
            mod_begin(0, 2, 1)
            steps = [0]

            def step(ins):
                steps[0] += 1
                ins.then_inc(pool_step, 1)
                pool.wait_ge(pool_step, steps[0])

            for l in range(DEPTH):
                if l == 0:
                    pool.wait_ge(h_ready, 4)
                    mod_begin(1, 0, 2)
                else:
                    pool.wait_ge(x_ready, 4)
                    mod_begin(1, 1, 3)
                    mod_begin(1, 2, 4)
                for t in range(2 * A_HEADS):
                    pool.wait_ge(sub_sum, 8 * l + t + 1)
                    rstd(g, step, SR, SS, 26, 1, 2 * HD)
                    g.tensor_copy(stat[:, SR:SR + 1], stat[:, SR:SR + 1]).then_inc(sub_rstd, 1)
            pool.wait_ge(hl_done, 1)
            pool.wait_ge(turned, 24)
            g.iota(iota_s[:], pattern=[[P, 2], [1, P]], base=0, channel_multiplier=0,
                   allow_small_or_imprecise_dtypes=True).then_inc(e_consts, 1)
            g.memset(pick_t[:].bitcast(F32), 0.0).then_inc(e_consts, 1)
            g.memset(table[:], 0.0).then_inc(e_consts, 1)
            g.memset(moe[:], 0.0).then_inc(e_consts, 1)

        @block.scalar
        def _(act):
            copy = ACT.Copy
            A = nc.scalar.activation
            def copy_part(a):
                n = a["n"]
                if plain_part(a["part"], n):
                    act.wait_ge(mod_mm, a["nth"] + 1)
                    A(mod[:, a["part"], n * 512:(n + 1) * 512], ps[:, a["odd_bank"], :], copy).then_inc(misc_read, 1)

            def squares(n):
                for i in range(NT):
                    if n == 0:
                        act.wait_ge(x_landed, 16)
                    else:
                        act.wait_ge(x_ready, 2 * (n - 1) + i + 1)
                    A(htok[:, i, :], x[:, i, :], ACT.Square, accum_out=stat[:, SQ + i:SQ + i + 1]).then_inc(sq_done, 1)

            loads = [
                (subg[:, 0, :], subln_g[0].partition_broadcast(P)),
                (subg[:, 1, :], subln_g[1].partition_broadcast(P)),
                (bf[:, 0, :], b_forget[0].partition_broadcast(P)),
                (bf[:, 1, :], b_forget[1].partition_broadcast(P)),
                (wf[:, 0], w_in[0, :, FC:GC].rearrange("(kb p) n -> p kb n", p=P)),
                (wf[:, 1], w_in[1, :, FC:GC].rearrange("(kb p) n -> p kb n", p=P)),
                (wr[:], w_router[0].rearrange("(kb p) n -> p kb n", p=P)),
                (buck[:], buckets), (block_sb[:], blocked),
            ]
            loads += [(lamv[:, l, k, :], v[l].partition_broadcast(P))
                      for l in range(DEPTH) for k, v in enumerate((lam_q1, lam_k1, lam_q2, lam_k2))]
            with nc.allow_non_contiguous_dma(reason="one small vector"):
                act.dma_start(cond[:], c[0].rearrange("(kb p) -> p kb", p=P)).then_inc(cond_landed, 16)
            act.wait_ge(cond_landed, 16)
            A(cs[:], cond[:], ACT.Silu).then_inc(cs_ready, 1)
            act.wait_ge(rel_cleared, 1)
            loads.append((rel[:, 0:N_BIAS], rel_bias))
            with nc.allow_non_contiguous_dma(reason="a few small parameters"):
                for dst, src in loads:
                    act.dma_start(dst, src).then_inc(consts_landed, 16)
            act.wait_ge(consts_landed, 16 * len(loads))
            A(wf_hi[:], wf[:], copy).then_inc(consts_split_hi, 1)
            A(wr_hi[:], wr[:], copy).then_inc(consts_split_hi, 1)
            act.wait_ge(consts_made, 10)
            A(ident_r[:], ident[:], copy).then_inc(ident_r_made, 1)
            act.wait_ge(lam_sum, 4)
            A(lam_s[:, :, 2:4], lam_s[:, :, 0:2], ACT.Exp).then_inc(lam_exp, 1)
            act.wait_ge(misc_read, 1)
            act.dma_start(scratch, vec[:]).then_inc(bias_rows, 16)
            squares(0)
            for kind, _, a, _ in plan.segments["start"][1]:
                if kind == "mod_sum":
                    copy_part(a)
            act.wait_ge(bias_rows, 16)

            def toeplitz(row, count):
                return bass.AP(scratch.tensor, row * NJ, [[1, P], [NJ, count], [1, S]])

            act.dma_start(bias[:, 0:2 * A_HEADS, :], toeplitz(0, 2 * A_HEADS)).then_inc(bias_landed, 16)
            for gr in range(G):
                r = 2 * A_HEADS
                act.dma_start(bias[:, r + gr:r + G * B_HEADS:G, :], toeplitz(r + gr * B_HEADS, B_HEADS))\
                    .then_inc(bias_landed, 16)
            act.dma_start(bias[:, N_BIAS:N_BIAS + 1, :], toeplitz(N_BIAS, 1)).then_inc(bias_landed, 16)

            def turn_high(k, scale=1.0):
                for n in range(4):
                    i, half = n // 2, n % 2
                    act.wait_ge(turned, 4 * k + n + 1)
                    A(ht_hi[:, 4 * half:4 * half + 4, i * P:(i + 1) * P],
                      ps[:, 2 + n, :].rearrange("p (k t) -> p k t", k=4), copy, scale=scale).then_inc(ht_high, 1)

            def high(u):
                act.wait_ge(raw_landed[u.raw], u.landed)
                if u.split >= H:
                    act.wait_ge(units_done, u.split - H + 1)
                A(unit_view(w_hi, u.hl, u), unit_view(raw, u.raw, u), copy).then_inc(high_done, 1)

            def mixer(l):
                first, ops = plan.segments[f"mix{l}"]
                for u in first:
                    if u.mod is None:
                        high(u)
                for kind, unit, a, ahead in ops:
                    highs = [u for u in ahead if u.mod is None]
                    own_first = kind in ("v", "gate") and a["last"]
                    for u in highs * (not own_first):
                        high(u)
                    if kind == "qk":
                        b, j, pair = a["bank"], a["j"], a["pair"]
                        if pair >= 2:
                            act.wait_ge(scores_done, len(tasks) * l + 2 * (pair - 1))
                        act.wait_ge(units_done, unit.split + 1)
                        A(qkt[:, pair % 2, j, :], ps[:, b, 0:S], copy, scale=HD ** -0.5 if j < 3 else 1.0)\
                            .then_inc(bank_read[b], 1)
                    elif kind == "v" and a["last"]:
                        for i in range(NT):
                            tile_done(act, i, unit, a)
                            A(vals[:, i, a["dst"]:a["dst"] + a["width"]], ps[:, i, 0:a["width"]], copy)\
                                .then_inc(bank_read[i], 1)
                    elif kind == "flip":
                        n = a["n"]
                        act.wait_ge(flip_mm, n + 1)
                        w_ = min(2 * S, (N_BIAS + 1) * S - n * 2 * S)
                        A(bias_flat[:, n * 2 * S:n * 2 * S + w_], ps[:, 2 + n % 4, 0:w_], copy).then_inc(flip_read, 1)
                        if n == FLIPS - 1:
                            act.wait_ge(flip_read, FLIPS)
                            act.dma_start(kept, bias[:, 0:2 * A_HEADS, :]).then_inc(bias_kept, 16)
                    elif kind == "gate" and a["last"]:
                        act.wait_ge(bias_kept, 16)
                        for i in range(NT):
                            tile_done(act, i, unit, a)
                            A(tanh_g[:, i, :], ps[:, i, :], ACT.Tanh, scale=0.5).then_inc(bank_read[i], 1)
                    elif kind == "forget":
                        act.wait_ge(forget_raw, l + 1)
                        A(ft[0:C_HEADS, :], ps[0:C_HEADS, 7, 0:S], copy).then_inc(misc_read, 1)
                    elif kind == "forget_turn":
                        act.wait_ge(forget_pre, l + 1)
                        A(lf_t[:, 2], lf_t[:, 1], ACT.Exp, scale=-1.0).then_inc(forget_exp, 1)
                        act.wait_ge(forget_exp, l + 1)
                        A(lf_t[:, 2], lf_t[:, 2], ACT.Ln, bias=1.0).then_inc(forget_ln, 1)
                    elif kind == "cumsum":
                        act.wait_ge(cum_mm, l + 1)
                        A(ft[0:C_HEADS, :], ps[0:C_HEADS, 7, 0:S], copy).then_inc(misc_read, 1)
                    elif kind == "mod_sum":
                        copy_part(a)
                    elif kind == "scores":
                        pair, i = tasks[a["t"]]
                        for half in range(2):
                            act.wait_ge(biased, 2 * a["n"] + half + 1)
                            view = by_map(prob[:, half], maps(pair), i)
                            A(view, view, ACT.Exp, scale=-1.0, bias=stat[:, NMAX + half:NMAX + half + 1],
                              accum_out=stat[:, DEN + half:DEN + half + 1]).then_inc(exp_done, 1)
                    elif kind == "turn_probs":
                        pair, i = tasks[a["t"]]
                        if a["n"]:
                            act.wait_ge(values_done, a["n"])
                        act.wait_ge(probs_turned, a["turned"] + 1)
                        width = maps(pair) * (i + 1) * P
                        A(prob_t[:, 0, 0:width], flat_scores(0)[:, 0:width], copy).then_inc(pt_low, 1)
                    elif kind == "turn_out":
                        _, i = tasks[a["t"]]
                        act.wait_ge(out_turned, a["n"] + 1)
                        A(ot_hi[:, a["t"] // 2, i * P:(i + 1) * P], ps[:, 7, 0:P], copy).then_inc(ot_high, 1)
                    elif kind == "turn_merged":
                        turn_high(1 + 3 * l, 0.5)
                    for u in highs * own_first:
                        high(u)

            def dense_high(k, it=0):
                slot, hl, before, s = dense_slots(k)
                act.wait_ge(raw_landed[slot], it * 16 + 16 * (before + 1))
                act.wait_ge(units_done, it * 6 + s - H + 1)
                A(w_hi[:, hl, :], raw[:, slot, :], copy).then_inc(high_done, 1)

            def dense_block(f, k, it=0, more=True):
                b = f % 2
                if more:
                    dense_high(k, it)
                act.wait_ge(units_done, it * 6 + dense_split0 + dense_index(f, "gate") + 1)
                A(silu_g[:, b, :], ps[:, 4 + b, 0:S], ACT.Silu).then_inc(d_silu, 1)
                if more:
                    dense_high(k + 1, it)
                act.wait_ge(d_prod, it * 2 + f + 1)
                A(act_hi[:, b, :], act_t[:, b, :], copy).then_inc(d_high, 1)
                dense_high(k + 2 if more else k, it)

            def dense():
                dense_high(0)
                dense_high(1)
                with act.Fori(0, DENSE_LOOPS) as it:
                    dense_block(0, 2, it)
                    dense_block(1, 5, it)
                k = 2 + 6 * DENSE_LOOPS
                dense_block(FB - 2, k)
                dense_block(FB - 1, k + 3, more=False)

            def experts(n):
                e0 = n * NE

                def unit(e, c, j):
                    k = j if isinstance(c, int) and c == 0 else j - 4
                    slot, hl = k % RE, k % HE
                    lap = (e + e0) * NC + c - (slot != k)
                    act.wait_ge(e_landed[slot], (lap + 1) * 16)
                    done = (e + e0) * EU + round_unit(c, j)
                    if not isinstance(done, int) or done >= HE:
                        act.wait_ge(e_used, done - HE + 1)
                    A(e_hi[:, hl, :], e_raw[:, slot, :], copy).then_inc(e_high, 1)

                def gathered(count):
                    act.wait_ge(e_gather, 2 * count - 1)
                    A(xg_hi[:], ps[:, 5:7, :].rearrange("p b (k t) -> p (b k) t", k=4), copy).then_inc(e_xhigh, 1)

                def hidden(count):
                    act.wait_ge(e_turned, count)
                    A(he_hi[:], ps[:, 2, :].rearrange("p (k t) -> p k t", k=4), copy).then_inc(e_hhigh, 1)

                def expert(e, fresh):
                    done = (e + e0) * EU
                    for j in range(5):
                        if not fresh:
                            unit(e, 0, j)
                    if fresh:
                        act.wait_ge(y_cleared, n + 1)
                    else:
                        act.wait_ge(e_used, done)
                    A(y_hi[:], ps[:, 3:5, :].rearrange("p b n -> p (b n)"), copy).then_inc(e_yhigh, 1)
                    for j in range(5, 8):
                        unit(e, 0, j)
                    act.wait_ge(e_used, done + 4)
                    A(silu_e[:], ps[:, 0, :], ACT.Silu).then_inc(e_silu, 1)
                    for j in range(LEAD):
                        unit(e, 1, j)
                    with act.Fori(1, NC) as c:
                        for j in range(LEAD, 9):
                            unit(e, c, j)
                        act.wait_ge(e_used, done + round_unit(c, 4))
                        act.wait_ge(e_prod, (e + e0) * NC + c)
                        A(silu_e[:], ps[:, 0, :], ACT.Silu).then_inc(e_silu, 1)
                        hidden((e + e0) * NC + c)
                        for j in range(9, 12):
                            unit(e, c, j)
                        for j in range(LEAD):
                            unit(e, c + 1, j)
                    unit(e, NC, 3)
                    hidden((e + e0) * NC + NC)
                    gathered(e + e0 + n + 2)

                for j in range(5):
                    if n == 0 and j == 2:
                        act.wait_ge(router_raw, 1)
                        A(ft[:], ps[0:NE, 7, 0:S], copy).then_inc(router_copied, 1)
                    if n == 0 and j == 3:
                        act.wait_ge(route_exp_in, 1)
                        A(route[:, 0, :, 1:2], route[:, 0, :, 0:1], ACT.Exp).then_inc(route_exp, 1)
                    unit(0, 0, j)
                gathered(n * (NE + 1) + 1)
                expert(0, True)
                with act.Fori(1, NE) as e:
                    expert(e, False)
                act.wait_ge(e_used, (NE + e0) * EU)
                A(y_hi[:], ps[:, 3:5, :].rearrange("p b n -> p (b n)"), copy).then_inc(e_yhigh, 1)

            for n, k in ((0, 0), (1, 2)):
                if n:
                    squares(n)
                turn_high(k)
                if n:
                    act.dma_start(bias[:, 0:2 * A_HEADS, :], kept).then_inc(bias_back, 16)
                mixer(0) if n == 0 else dense()
            for n, k in ((2, 3), (3, 5)):
                squares(n)
                turn_high(k)
                if n == 2:
                    mixer(1)
            act.wait_ge(h_ready, 16)
            A(hh[:], htok[:], copy).then_inc(hh_done, 1)
            act.wait_ge(units_done, plan.split_n)
            act.wait_ge(low_done, plan.split_n)
            experts(0)
            act.wait_ge(flag_done, 1)
            more = act.value_load(flag[0:1, 0:1], min_val=0, max_val=1)
            with act.If(more > 0):
                experts(1)
            for i in range(NT):
                act.wait_ge(h_final, i + 1)
                A(moe[:, i, :], x[:, i, :], ACT.Square, accum_out=stat[:, SQ + i:SQ + i + 1]).then_inc(final_sq, 1)

        @block.tensor
        def _(pe):
            mm = pe.matmul

            def product(dst, lhs, rhs, start, stop):
                mm(dst, lhs[0], rhs[0], start=start, stop=False)
                mm(dst, lhs[0], rhs[1], start=False, stop=False)
                return mm(dst, lhs[1], rhs[0], start=False, stop=stop)

            NORMS = (0, 2, 3, 5)

            def turn(k, src):
                for n in range(4):
                    i, half = n // 2, n % 2
                    if k in NORMS:
                        pe.wait_ge(h_ready, 4 * NORMS.index(k) + n + 1)
                    elif half == 0:
                        pe.wait_ge(merged_done, 8 * (k // 3) + 7 + i)
                    for j in range(4):
                        kb = 4 * half + j
                        last = pe.transpose(ps[:, 2 + n, j * P:(j + 1) * P], src[:, i, kb * P:(kb + 1) * P], ident[:])
                    last.then_inc(turned, 1)

            def thin(n, hi, lo):
                for kb in range(KB):
                    last = product(ps[0:n, 7, 0:S], (hi[:, kb, :], lo[:, kb, :]), (ht_hi[:, kb, :], ht_lo[:, kb, :]),
                                   kb == 0, kb == KB - 1)
                return last

            def thin_turn(n):
                for i in range(NT):
                    last = pe.transpose(ps[:, 7, n * i:n * (i + 1)], ft[0:n, i * P:(i + 1) * P], ident[0:n, 0:n])
                return last

            def mixer(l):
                _, ops = plan.segments[f"mix{l}"]
                for kind, unit, a, _ in ops:
                    if unit is not None and unit.mod is None:
                        pe.wait_ge(low_done, unit.split + 1)
                        wh, wl = unit_view(w_hi, unit.hl, unit), unit_view(w_lo, unit.hl, unit)
                    if kind == "qk":
                        b = a["bank"]
                        if a["uses"]:
                            pe.wait_ge(bank_read[b], a["uses"])
                        for kb in range(KB):
                            last = product(ps[:, b, 0:S], (wh[:, kb, :], wl[:, kb, :]),
                                           (ht_hi[:, kb, :], ht_lo[:, kb, :]), kb == 0, kb == KB - 1)
                        last.then_inc(units_done, 1)
                    elif kind in ("v", "gate", "lift", "out"):
                        off, hi, lo = 0, ht_hi, ht_lo
                        if kind == "lift":
                            off, hi, lo = (0, 4, 7)[a["b"]], ot_hi, ot_lo
                        if a["first"]:
                            if kind == "lift":
                                pe.wait_ge(misc_read, a["outs"])
                        nk, width = unit.shape
                        for i in range(NT):
                            if kind == "out" and a["n"] == 0 and a["first"]:
                                pe.wait_ge(ht_low, 4 * (3 * l + 1) + 2 * (i + 1))
                            if a["first"] and a["uses"][i]:
                                pe.wait_ge(bank_read[i], a["uses"][i])
                            for k in range(nk):
                                tok = slice(i * P, (i + 1) * P)
                                last = product(ps[:, i, 0:width],
                                               (hi[:, off + a["k0"] + k, tok], lo[:, off + a["k0"] + k, tok]),
                                               (wh[:, k, :], wl[:, k, :]), a["first"] and k == 0,
                                               a["last"] and k == nk - 1)
                            if a["last"] and i == 0:
                                last.then_inc(tile0_done, 1)
                        last.then_inc(units_done, 1)
                    elif kind == "forget":
                        pe.wait_ge(misc_read, a["misc"])
                        pe.wait_ge(consts_split_lo, 2)
                        pe.wait_ge(ht_low, 4 * (3 * l + 1))
                        thin(C_HEADS, wf_hi[:, l], wf_lo[:, l]).then_inc(forget_raw, 1)
                    elif kind == "forget_turn":
                        pe.wait_ge(misc_read, a["misc"])
                        thin_turn(C_HEADS).then_inc(forget_mm, 1)
                    elif kind == "cumsum":
                        pe.wait_ge(misc_read, a["misc"])
                        pe.wait_ge(forget_log, l + 1)
                        for i in range(NT):
                            last = mm(ps[0:C_HEADS, 7, 0:S], lf[:, i, :], tri[:, i, :], start=i == 0, stop=i == NT - 1)
                        last.then_inc(cum_mm, 1)
                    elif kind == "mod_sum":
                        sum_part(a)
                    elif kind == "flip":
                        n = a["n"]
                        if n == 0:
                            pe.wait_ge(bias_landed, 16 * 5)
                        if n >= 4:
                            pe.wait_ge(flip_read, n - 3)
                        w_ = min(2 * S, (N_BIAS + 1) * S - n * 2 * S)
                        mm(ps[:, 2 + n % 4, 0:w_], anti[:], bias_flat[:, n * 2 * S:n * 2 * S + w_], start=True,
                           stop=True).then_inc(flip_mm, 1)
                    elif kind == "scores":
                        pair, i = tasks[a["t"]]
                        n = maps(pair)
                        if a["t"] == 0:
                            pe.wait_ge(flip_read, FLIPS)
                        for b in range(2):
                            pe.wait_ge(bank_read[b], a["ready"][b])
                        if a["n"]:
                            pe.wait_ge(biased, 2 * a["n"])
                            pe.wait_ge(pt_low, a["n"])
                            if a["upper"]:
                                pe.wait_ge(pt_up, a["upper"])
                        if pair >= 7:
                            pe.wait_ge(misc_read, a["cumsum"])
                        K = (i + 1) * P
                        for half in range(2):
                            rows = slice(HD * half, HD * (half + 1))
                            for m in range(n):
                                dst = flat_scores(half)[:, m * S:m * S + K]
                                last = mm(dst, qkt[rows, pair % 2, m, i * P:(i + 1) * P],
                                          qkt[rows, pair % 2, 3 + m, 0:K], start=True, stop=pair < 7)
                        if pair >= 7:
                            for half in range(2):
                                h = 2 * (pair - 7) + half
                                dst = flat_scores(half)[:, 0:K]
                                mm(dst, ft[0:C_HEADS, i * P:(i + 1) * P], ident[0:C_HEADS, h:h + 1].to_broadcast([C_HEADS, K]),
                                   start=False, stop=False)
                                last = mm(dst, neg_ident[0:C_HEADS, h:h + 1].to_broadcast([C_HEADS, P]), ft[0:C_HEADS, 0:K],
                                          start=False, stop=True)
                        last.then_inc(scores_done, 1)
                    elif kind == "turn_probs":
                        pair, i = tasks[a["t"]]
                        for half in range(1 + (pair >= 4)):
                            if pair < 4:
                                pe.wait_ge(diff_done, 8 * l + a["t"] + 1)
                            else:
                                pe.wait_ge(exp_done, 2 * a["n"] + half + 1)
                            for m in range(maps(pair)):
                                for kb in range(i + 1):
                                    at_ = (m * (i + 1) + kb) * P
                                    last = pe.transpose(flat_scores(half)[:, at_:at_ + P],
                                                        prob[:, half, m * S + kb * P:m * S + (kb + 1) * P], ident[:])
                            last.then_inc(probs_turned, 1)
                    elif kind == "values":
                        pair, i = tasks[a["t"]]
                        n = maps(pair)
                        pe.wait_ge(pt_low, a["n"] + 1)
                        if pair >= 4:
                            pe.wait_ge(pt_up, a["upper"])
                        for b in range(2):
                            pe.wait_ge(bank_read[b], a["ready"][b])
                        if a["n"]:
                            pe.wait_ge(o_taken, a["n"])
                        for half in range(1 + (pair >= 4)):
                            width = P if pair < 4 else HD
                            dst = ps[:, 6, half * HD:half * HD + width]
                            steps = [(m, kb) for m in range(n) for kb in range(i + 1)]
                            for s_, (m, kb) in enumerate(steps):
                                if pair < 4:
                                    col = P * pair
                                elif pair < 7:
                                    col = A_W + m * B_W + HD * (2 * (pair - 4) + half)
                                else:
                                    col = A_W + G * B_W + HD * (2 * (pair - 7) + half)
                                at_ = (m * (i + 1) + kb) * P
                                last = mm(dst, prob_t[:, half, at_:at_ + P], vals[:, kb, col:col + width],
                                          start=s_ == 0, stop=s_ == len(steps) - 1)
                        last.then_inc(values_done, 1)
                    elif kind == "turn_out":
                        pe.wait_ge(misc_read, a["misc"])
                        if tasks[a["t"]][0] < 4:
                            pe.wait_ge(o_normed, 8 * l + a["t"] + 1)
                        else:
                            pe.wait_ge(o_taken, a["n"] + 1)
                        pe.transpose(ps[:, 7, 0:P], o_tok[:, a["t"] % 2, :], ident[:]).then_inc(out_turned, 1)
                    elif kind == "turn_merged":
                        turn(1 + 3 * l, merged)

            def sum_part(a):
                n = a["n"]
                pe.wait_ge(mod_used, 16 * (a["nth"] // 4 + 1))
                if a["odd_bank"] == 7:
                    pe.wait_ge(misc_read, a["misc"])
                mm(ps[:, a["odd_bank"], :], ones[:], mod[:, a["part"], n * 512:(n + 1) * 512], start=True, stop=True)\
                    .then_inc(mod_mm, 1)

            def dense():
                pe.wait_ge(ht_low, 12)
                for n in range(4):
                    mm(ps[:, n, :], zero_r[:], ht_hi[:, 0:2, :].rearrange("p k t -> p (k t)"), start=True, stop=False)

                def up(k, f, it=0):
                    for j in range(2):
                        _, hl, _, s = dense_slots(k + j)
                        pe.wait_ge(low_done, it * 6 + s + 1)
                        if j == 0 and not (isinstance(it, int) and f < 2):
                            pe.wait_ge(d_prod, it * 2 + f - 1)
                        for kb in range(KB):
                            last = product(ps[:, 4 + 2 * j + f % 2, 0:S],
                                           (w_hi[:, hl, kb * P:(kb + 1) * P], w_lo[:, hl, kb * P:(kb + 1) * P]),
                                           (ht_hi[:, kb, :], ht_lo[:, kb, :]), kb == 0, kb == KB - 1)
                        last.then_inc(units_done, 1)

                def down(k, f, it=0, stop=False):
                    _, hl, _, s = dense_slots(k)
                    pe.wait_ge(low_done, it * 6 + s + 1)
                    pe.wait_ge(d_low, it * 2 + f + 1)
                    for i in range(NT):
                        if stop and i:
                            last.then_inc(d_tile0, 1)
                        for n in range(2):
                            tok = slice(i * P, (i + 1) * P)
                            last = product(ps[:, 2 * i + n, :], (act_hi[:, f % 2, tok], act_lo[:, f % 2, tok]),
                                           (w_hi[:, hl, n * 512:(n + 1) * 512], w_lo[:, hl, n * 512:(n + 1) * 512]),
                                           False, stop)
                    last.then_inc(units_done, 1)

                up(0, 0)
                up(2, 1)
                down(4, 0)
                up(5, 2)
                down(7, 1)
                with pe.Fori(1, DENSE_LOOPS) as it:
                    up(2, 1, it)
                    down(4, 0, it)
                    up(5, 2, it)
                    down(7, 1, it)
                k = 2 + 6 * DENSE_LOOPS
                up(k, FB - 1)
                down(k + 2, FB - 2)
                down(k + 3, FB - 1, stop=True)

            def router():
                pe.wait_ge(ht_low, 24)
                thin(NE, wr_hi, wr_lo).then_inc(router_raw, 1)
                pe.wait_ge(router_copied, 1)
                thin_turn(NE).then_inc(router_mm, 1)
                pe.wait_ge(member_done, 1)
                for i in range(NT):
                    for j in range(i + 1):
                        mm(ps[:, 7, NE * i:NE * (i + 1)], tri[:, j, i * P:(i + 1) * P], route[:, 4, j, :],
                           start=j == 0, stop=j == i)
                for j in range(NT):
                    last = mm(ps[:, 7, 2 * NE:3 * NE], ones[:], route[:, 4, j, :], start=j == 0, stop=j == NT - 1)
                last.then_inc(rank_mm, 1)

            def experts(n):
                e0 = n * NE

                def split_unit(e, c, j):
                    pe.wait_ge(e_low, (e + e0) * EU + round_unit(c, j) + 1)
                    hl = (j if isinstance(c, int) and c == 0 else j - 4) % HE
                    return e_hi[:, hl, :], e_lo[:, hl, :]

                def hidden(bank, e, c, j0):
                    for j in range(4):
                        wh, wl = split_unit(e, c, j0 + j)
                        for k in range(2):
                            kb = 2 * j + k
                            last = product(ps[:, bank, :], (xg_hi[:, kb, :], xg_lo[:, kb, :]),
                                           (wh[:, k * CH:(k + 1) * CH], wl[:, k * CH:(k + 1) * CH]),
                                           kb == 0, kb == KB - 1)
                        last.then_inc(e_used, 1)

                def turn_hidden(count):
                    pe.wait_ge(e_prod, count)
                    for j in range(4):
                        last = pe.transpose(ps[:, 2, j * P:(j + 1) * P], h_e[:, j * P:(j + 1) * P], ident[:])
                    last.then_inc(e_turned, 1)

                def down(e, c, j0, stop=False):
                    pe.wait_ge(e_hlow, (e + e0) * NC + c)
                    for j in range(4):
                        wh, wl = split_unit(e, c, j0 + j)
                        for h in range(2):
                            cols = slice(h * 512, (h + 1) * 512)
                            last = product(ps[:, 3 + h, :], (he_hi[:, j, :], he_lo[:, j, :]),
                                           (wh[:, cols], wl[:, cols]), False, stop and j == 3)
                        last.then_inc(e_used, 1)

                def gather(count):
                    pe.wait_ge(e_pick, NT * count)
                    for part, src, banks in ((0, hh, (5, 6)), (1, hl, (7, 0))):
                        for kb in range(KB):
                            for i in range(NT):
                                last = mm(ps[:, banks[kb // 4], (kb % 4) * P:(kb % 4 + 1) * P],
                                          src[:, i, kb * P:(kb + 1) * P], pick[:, i, :], start=i == 0, stop=i == NT - 1)
                        last.then_inc(e_gather, 1)

                def scatter(count):
                    pe.wait_ge(e_ylow, count)
                    for i in range(NT):
                        for h in range(2):
                            bank = BACK[2 * i + h]
                            mm(ps[:, bank, :], pick_t[:, i, :], y_hi[:, h * 512:(h + 1) * 512], start=True, stop=False)
                            mm(ps[:, bank, :], pick_t[:, i, :], y_lo[:, h * 512:(h + 1) * 512], start=False, stop=True)\
                                .then_inc(e_back, 1)

                def turn_pick():
                    for i in range(NT):
                        last = mm(ps[:, 7, i * P:(i + 1) * P], pick[:, i, :], ident_r[:], start=True, stop=True)
                    last.then_inc(e_pick_turned, 1)

                def expert(e):
                    pe.wait_ge(e_xhigh, (e + e0) + n + 1)
                    pe.wait_ge(e_xlow, ((e + e0) + n + 1) * 2)
                    hidden(0, e, 0, 0)
                    scatter((e + e0) + n + 1)
                    for h in range(2):
                        mm(ps[:, 3 + h, :], zero_r[:], xg_hi[:, 0:4, :].rearrange("p k t -> p (k t)"), start=True, stop=False)
                    if not (isinstance(e, int) and e + e0 == 0):
                        pe.wait_ge(e_prod, (e + e0) * NC)
                    hidden(1, e, 0, 4)
                    pe.wait_ge(e_back_read, ((e + e0) + n + 1) * 4)
                    turn_pick()
                    with pe.Fori(1, NC) as c:
                        chunks = (e + e0) * NC + c
                        pe.wait_ge(e_silu, chunks)
                        hidden(0, e, c, 0)
                        turn_hidden(chunks)
                        hidden(1, e, c, 4)
                        down(e, c, 8)
                    turn_hidden((e + e0) * NC + NC)
                    pe.wait_ge(e_silu, (e + e0) * NC + NC)
                    gather((e + e0) + n + 2)
                    down(e, NC, 0, stop=True)

                gather(e0 + n + 1)
                expert(0)
                with pe.Fori(1, NE) as e:
                    expert(e)
                scatter(e0 + n + NE + 1)

            pe.wait_ge(consts_landed, 16 * N_LOADS)
            mm(ps[0:N_BIAS + 1, 7, 0:NJ], rel[:], buck[:], start=True, stop=True).then_inc(bias_prod, 1)
            pe.wait_ge(consts_made, 10)
            for kind, unit, a, _ in plan.segments["start"][1]:
                if kind == "mod_sum":
                    sum_part(a)
            turn(0, htok)
            mixer(0)
            turn(2, htok)
            dense()
            turn(3, htok)
            mixer(1)
            turn(5, htok)
            router()
            pe.wait_ge(ident_r_made, 1)
            experts(0)
            pe.wait_ge(flag_done, 1)
            more = pe.value_load(flag[0:1, 0:1], min_val=0, max_val=1)
            with pe.If(more > 0):
                experts(1)

        @block.vector
        def _(dve):
            V = nc.vector
            STT, TT, TS = V.scalar_tensor_tensor, V.tensor_tensor, V.tensor_scalar
            count = [0]

            def step(ins):
                count[0] += 1
                ins.then_inc(dve_step, 1)
                dve.wait_ge(dve_step, count[0])

            def norm_factor(n):
                dve.wait_ge(sq_done, 2 * n + 2)
                rstd(V, step, RS, SQ, 20, NT, D)

            def modulate(n, a_, b_):
                if n:
                    norm_factor(n)
                for i in range(NT):
                    for half in range(2):
                        c_ = slice(half * 512, (half + 1) * 512)
                        step(STT(htok[:, i, c_], x[:, i, c_], stat[:, RS + i:RS + i + 1], a_[:, c_], ALU.mult,
                                 ALU.mult))
                        TT(htok[:, i, c_], htok[:, i, c_], b_[:, c_], ALU.add).then_inc(h_ready, 1)

            def turn_low(k, scale=1.0):
                for n in range(4):
                    i, half = n // 2, n % 2
                    dve.wait_ge(ht_high, 4 * k + n + 1)
                    at_ = (slice(None), slice(4 * half, 4 * half + 4), slice(i * P, (i + 1) * P))
                    STT(ht_lo[at_], ps[:, 2 + n, :].rearrange("p (k t) -> p k t", k=4), scale,
                        ht_hi[at_].bitcast(F32), ALU.mult, ALU.subtract).then_inc(ht_low, 1)

            def use(u):
                if u.mod is None:
                    dve.wait_ge(high_done, u.split + 1)
                    TT(unit_view(w_lo, u.hl, u), unit_view(raw, u.raw, u), unit_view(w_hi, u.hl, u).bitcast(F32),
                       ALU.subtract).then_inc(low_done, 1)
                    return
                l, part, kb, half = u.mod
                dve.wait_ge(raw_landed[u.raw], u.landed)
                if kb == 0 and half == 0:
                    dve.wait_ge(mod_start[l][part], 16)
                if kb:
                    dve.wait_ge(mod_used, u.nth - 1)
                acc = mod[:, part, half * UM:(half + 1) * UM]
                STT(acc, raw[:, u.raw, :], cs[:, kb:kb + 1], acc, ALU.mult, ALU.add).then_inc(mod_used, 1)

            def scale_part(a):
                n = a["n"]
                if not plain_part(a["part"], n):
                    dve.wait_ge(gain_landed, 16 * (2 * a["l"] + (a["part"] == 2) + 1))
                    dve.wait_ge(mod_mm, a["nth"] + 1)
                    STT(mod[:, a["part"], n * 512:(n + 1) * 512], ps[:, a["odd_bank"], :], 1.0,
                        gain[:, (n % 2) * 512:(n % 2 + 1) * 512], ALU.add, ALU.mult).then_inc(misc_read, 1)

            def mixer(l):
                first, ops = plan.segments[f"mix{l}"]
                for u in first:
                    use(u)
                for kind, unit, a, ahead in ops:
                    own_first = kind in ("lift", "out") and a["last"]
                    for u in ahead * (not own_first):
                        use(u)
                    if kind == "forget_turn":
                        dve.wait_ge(forget_mm, l + 1)
                        for i in range(NT):
                            z = TT(lf_t[:, 0, i, :], ps[:, 7, C_HEADS * i:C_HEADS * (i + 1)], bf[:, l, :], ALU.add)
                            z.then_inc(misc_read, 1) if i == NT - 1 else step(z)
                        dve.wait_ge(misc_read, a["misc"] + 1)
                        STT(lf_t[:, 1], lf_t[:, 0], -1.0, lf_t[:, 0], ALU.mult, ALU.max).then_inc(forget_pre, 1)
                        dve.wait_ge(forget_ln, l + 1)
                        STT(lf[:], lf_t[:, 0], 0.0, lf_t[:, 2], ALU.min, ALU.subtract).then_inc(forget_log, 1)
                    elif kind == "mod_sum":
                        scale_part(a)
                    elif kind == "scores":
                        pair, i = tasks[a["t"]]
                        n = maps(pair)
                        dve.wait_ge(scores_done, a["n"] + 1)
                        if a["t"] == 0:
                            dve.wait_ge(flip_read, FLIPS)
                            if l:
                                dve.wait_ge(bias_back, 16)
                        for half in range(2):
                            r = bias_of(pair, half)
                            V.tensor_tensor_reduce(by_map(prob[:, half], n, i), by_map(flat_scores(half), n, i),
                                                   bias[:, r:r + n, P * (1 - i):S], -1.0, 3e38, ALU.add, ALU.min,
                                                   stat[:, NMAX + half:NMAX + half + 1]).then_inc(biased, 1)
                    elif kind == "weigh":
                        pair, i = tasks[a["t"]]
                        RDEN = RDENS[a["t"] % 2]
                        dve.wait_ge(exp_done, 2 * a["n"] + 2)
                        step(V.reciprocal(stat[:, RDEN:RDEN + 2], stat[:, DEN:DEN + 2]))
                        if pair < 4:
                            step(STT(stat[:, COEF:COEF + 1], stat[:, DEN:DEN + 1], stat[:, RDEN + 1:RDEN + 2],
                                     neg_lam[:, l:l + 1], ALU.mult, ALU.mult))
                            K = (i + 1) * P
                            STT(prob[:, 0, 0:K], prob[:, 1, 0:K], stat[:, COEF:COEF + 1], prob[:, 0, 0:K],
                                ALU.mult, ALU.add).then_inc(diff_done, 1)
                    elif kind == "turn_probs":
                        pair, i = tasks[a["t"]]
                        if pair >= 4:
                            if a["n"]:
                                dve.wait_ge(values_done, a["n"])
                            dve.wait_ge(probs_turned, a["turned"] + 2)
                            width = maps(pair) * (i + 1) * P
                            V.tensor_copy(prob_t[:, 1, 0:width], flat_scores(1)[:, 0:width]).then_inc(pt_up, 1)
                    elif kind == "finish":
                        pair, i = tasks[a["t"]]
                        RDEN = RDENS[a["t"] % 2]
                        o = o_tok[:, a["t"] % 2, :]
                        dve.wait_ge(values_done, a["n"] + 1)
                        if pair < 4:
                            TS(o, ps[:, 6, 0:P], stat[:, RDEN:RDEN + 1], None, ALU.mult).then_inc(o_taken, 1)
                            dve.wait_ge(o_taken, a["n"] + 1)
                            V.tensor_tensor_reduce(o_tok[:, (a["t"] + 1) % 2, :], o, o, 1.0, 0.0, ALU.mult, ALU.add,
                                                   stat[:, SS:SS + 1]).then_inc(sub_sum, 1)
                        else:
                            for half in range(2):
                                cols = slice(half * HD, (half + 1) * HD)
                                ins = TS(o[:, cols], ps[:, 6, cols], stat[:, RDEN + half:RDEN + half + 1], None, ALU.mult)
                                ins.then_inc(o_taken, 1) if half else step(ins)
                    elif kind == "norm_out" and tasks[a["t"]][0] < 4:
                        o = o_tok[:, a["t"] % 2, :]
                        dve.wait_ge(sub_rstd, 8 * l + a["t"] + 1)
                        STT(o, o, stat[:, SR:SR + 1], subg[:, l, :], ALU.mult, ALU.mult).then_inc(o_normed, 1)
                    elif kind == "turn_out":
                        _, i = tasks[a["t"]]
                        dve.wait_ge(ot_high, a["n"] + 1)
                        at_ = (slice(None), a["t"] // 2, slice(i * P, (i + 1) * P))
                        TT(ot_lo[at_], ps[:, 7, 0:P], ot_hi[at_].bitcast(F32), ALU.subtract).then_inc(misc_read, 1)
                    elif kind == "lift" and a["last"]:
                        for i in range(NT):
                            tile_done(dve, i, unit, a)
                            cols = slice(a["n"] * 512, (a["n"] + 1) * 512)
                            dve.wait_ge(bank_read[i], a["uses"][i])
                            if a["b"] == 0:
                                STT(merged[:, i, cols], tanh_g[:, i, :], 1.0, ps[:, i, :], ALU.add, ALU.mult)\
                                    .then_inc(bank_read[i], 1)
                                dve.wait_ge(bank_read[i], a["uses"][i] + 1)
                            else:
                                STT(lifted[:], tanh_g[:, i, :], 1.0, ps[:, i, :], ALU.add, ALU.mult)\
                                    .then_inc(bank_read[i], 1)
                                dve.wait_ge(bank_read[i], a["uses"][i] + 1)
                                TT(merged[:, i, cols], merged[:, i, cols], lifted[:], ALU.add).then_inc(merged_done, 1)
                                dve.wait_ge(merged_done, 8 * l + 4 * (a["b"] - 1) + 2 * a["n"] + i + 1)
                    elif kind == "turn_merged":
                        turn_low(1 + 3 * l, 0.5)
                    elif kind == "out" and a["last"]:
                        dve.wait_ge(misc_read, plan.part_ready[l, 1])
                        for i in range(NT):
                            tile_done(dve, i, unit, a)
                            cols = slice(a["n"] * 512, (a["n"] + 1) * 512)
                            TT(lifted[:], ps[:, i, :], G1[:, cols], ALU.mult).then_inc(bank_read[i], 1)
                            dve.wait_ge(bank_read[i], a["uses"][i] + 1)
                            ins = TT(x[:, i, cols], x[:, i, cols], lifted[:], ALU.add)
                            if a["n"] == 0:
                                step(ins)
                            else:
                                ins.then_inc(x_ready, 1)
                                dve.wait_ge(x_ready, 4 * l + i + 1)
                    for u in ahead * own_first:
                        use(u)

            def dense():
                def low(k, it=0):
                    slot, hl, _, s = dense_slots(k)
                    dve.wait_ge(high_done, it * 6 + s + 1)
                    TT(w_lo[:, hl, :], raw[:, slot, :], w_hi[:, hl, :].bitcast(F32), ALU.subtract).then_inc(low_done, 1)

                def block_(f, k, it=0, more=True):
                    b = f % 2
                    if more:
                        low(k, it)
                    dve.wait_ge(units_done, it * 6 + dense_split0 + dense_index(f, "up") + 1)
                    dve.wait_ge(d_silu, it * 2 + f + 1)
                    TT(act_t[:, b, :], silu_g[:, b, :], ps[:, 6 + b, 0:S], ALU.mult).then_inc(d_prod, 1)
                    if more:
                        low(k + 1, it)
                    dve.wait_ge(d_high, it * 2 + f + 1)
                    TT(act_lo[:, b, :], act_t[:, b, :], act_hi[:, b, :].bitcast(F32), ALU.subtract).then_inc(d_low, 1)
                    low(k + 2 if more else k, it)

                low(0)
                low(1)
                with dve.Fori(0, DENSE_LOOPS) as it:
                    block_(0, 2, it)
                    block_(1, 5, it)
                k = 2 + 6 * DENSE_LOOPS
                block_(FB - 2, k)
                block_(FB - 1, k + 3, more=False)
                for i in range(NT):
                    if i == 0:
                        dve.wait_ge(d_tile0, 1)
                    else:
                        dve.wait_ge(units_done, dense_split0 + 3 * FB)
                    for n in range(2):
                        cols = slice(n * 512, (n + 1) * 512)
                        step(TT(upd[:], ps[:, 2 * i + n, :], G2[:, cols], ALU.mult))
                        ins = TT(x[:, i, cols], x[:, i, cols], upd[:], ALU.add)
                        if n == 0:
                            step(ins)
                        else:
                            ins.then_inc(x_ready, 1)
                            dve.wait_ge(x_ready, 2 + i + 1)

            def routing(meanwhile):
                dve.wait_ge(router_mm, 1)
                dve.wait_ge(e_consts, 4)
                L = route[:, 5]
                step(V.tensor_copy(L, ps[:, 7, 0:NT * NE].rearrange("p (i e) -> p i e", i=NT)))
                for i in range(NT):
                    step(V.max(top_v[:, i, :], L[:, i, :]))
                    step(V.max_index(top_i[:, i, :], top_v[:, i, :], L[:, i, :]))
                step(V.tensor_copy(top_f[:], top_i[:]))
                TT(route[:, 0, :, 0:1], top_v[:, :, 1:2], top_v[:, :, 0:1], ALU.subtract).then_inc(route_exp_in, 1)
                dve.wait_ge(route_exp, 1)
                step(TS(route[:, 0, :, 2:3], route[:, 0, :, 1:2], 1.0, None, ALU.add))
                step(V.reciprocal(route[:, 0, :, 3:4], route[:, 0, :, 2:3]))
                step(TT(route[:, 0, :, 4:5], route[:, 0, :, 3:4], route[:, 0, :, 1:2], ALU.mult))
                for i in range(NT):
                    for j in range(2):
                        step(TS(route[:, 1 + j, i, :], iota_s[:, 0, 0:NE], top_f[:, i, j:j + 1], None, ALU.is_equal))
                    step(TS(route[:, 3, i, :], route[:, 1, i, :], route[:, 0, i, 3:4], None, ALU.mult))
                    step(STT(table[:, 2, i, 1:NE + 1], route[:, 2, i, :], route[:, 0, i, 4:5], route[:, 3, i, :],
                             ALU.mult, ALU.add))
                step(TT(table[:, 1, :, 1:NE + 1], route[:, 1], route[:, 2], ALU.add))
                V.tensor_copy(route[:, 4], table[:, 1, :, 1:NE + 1]).then_inc(member_done, 1)
                meanwhile()
                dve.wait_ge(rank_mm, 1)
                dve.wait_ge(member_done, 1)
                step(TT(table[:, 0, :, 1:NE + 1], ps[:, 7, 0:NT * NE].rearrange("p (i e) -> p i e", i=NT), route[:, 4],
                        ALU.subtract))
                step(V.tensor_reduce(flag_f[:], ps[:, 7, 2 * NE:3 * NE], AX_X, ALU.max))
                TS(flag[:], flag_f[:], float(P), None, ALU.is_gt).then_inc(flag_done, 1)

            def experts(n):
                e0 = n * NE

                def low(e, c, j):
                    k = j if isinstance(c, int) and c == 0 else j - 4
                    dve.wait_ge(e_high, (e + e0) * EU + round_unit(c, j) + 1)
                    TT(e_lo[:, k % HE, :], e_raw[:, k % RE, :], e_hi[:, k % HE, :].bitcast(F32), ALU.subtract)\
                        .then_inc(e_low, 1)

                def hidden_low(count):
                    dve.wait_ge(e_hhigh, count)
                    TT(he_lo[:], ps[:, 2, :].rearrange("p (k t) -> p k t", k=4), he_hi[:].bitcast(F32), ALU.subtract)\
                        .then_inc(e_hlow, 1)

                def gathered_low(count):
                    dve.wait_ge(e_gather, 2 * count)
                    V.tensor_copy(xg_lo[:, 0:4, :], ps[:, 7, :].rearrange("p (k t) -> p k t", k=4)).then_inc(e_xlow, 1)
                    V.tensor_copy(xg_lo[:, 4:8, :], ps[:, 0, :].rearrange("p (k t) -> p k t", k=4)).then_inc(e_xlow, 1)

                def pick_for(e):
                    for i in range(NT):
                        ins = TS(pick[:, i, :], iota_s[:, n, :], table[:, 0, i, bass.ds(e + 1, 1)],
                                 table[:, 1, i, bass.ds(e + 1, 1)], ALU.is_equal, ALU.mult)
                        ins.then_inc(e_pick, 1)

                def y_low(count):
                    dve.wait_ge(e_yhigh, count)
                    TT(y_lo[:], ps[:, 3:5, :].rearrange("p b n -> p (b n)"), y_hi[:].bitcast(F32), ALU.subtract)\
                        .then_inc(e_ylow, 1)

                def add_back(e, count):
                    for i in range(NT):
                        for h in range(2):
                            k = 2 * i + h
                            dve.wait_ge(e_back, (count - 1) * 4 + k + 1)
                            cols = slice(h * 512, (h + 1) * 512)
                            STT(moe[:, i, cols], ps[:, BACK[k], :], table[:, 2, i, bass.ds(e, 1)], moe[:, i, cols],
                                ALU.mult, ALU.add).then_inc(e_back_read, 1)

                def prod(count):
                    dve.wait_ge(e_silu, count)
                    TT(h_e[:], silu_e[:], ps[:, 1, :], ALU.mult).then_inc(e_prod, 1)

                def expert(e, first=False):
                    done = (e + e0) * EU
                    for j in range(5):
                        if not first:
                            low(e, 0, j)
                    y_low((e + e0) + n + 1)
                    for j in range(5, 8):
                        low(e, 0, j)
                    add_back(e, (e + e0) + n + 1)
                    for j in range(LEAD):
                        low(e, 1, j)
                    dve.wait_ge(e_used, done + 8)
                    prod((e + e0) * NC + 1)
                    dve.wait_ge(e_pick_turned, (e + e0) + 1)
                    V.tensor_copy(pick_t[:], ps[:, 7, 0:NT * P].rearrange("p (i t) -> p i t", i=NT))
                    pick_for(e + 1)
                    with dve.Fori(1, NC) as c:
                        for j in range(LEAD, 9):
                            low(e, c, j)
                        hidden_low((e + e0) * NC + c)
                        for j in range(9, 12):
                            low(e, c, j)
                        dve.wait_ge(e_used, done + round_unit(c, 8))
                        prod((e + e0) * NC + c + 1)
                        for j in range(LEAD):
                            low(e, c + 1, j)
                    low(e, NC, 3)
                    hidden_low((e + e0) * NC + NC)
                    gathered_low((e + e0) + n + 2)

                dve.wait_ge(ht_low, 24)
                V.memset(ps[:, 3:5, :], 0.0).then_inc(y_cleared, 1)
                if n == 0:
                    for j in range(2):
                        low(0, 0, j)
                    routing(lambda: [low(0, 0, j) for j in (2, 3)])
                pick_for(0)
                for j in range(4 * (n == 0), 5):
                    low(0, 0, j)
                gathered_low(e0 + n + 1)
                expert(0, True)
                with dve.Fori(1, NE) as e:
                    expert(e)
                y_low(e0 + n + NE + 1)
                add_back(NE, e0 + n + NE + 1)
                dve.wait_ge(e_back_read, (NE + 1) * 4 * (n + 1))

            def small_parameters():
                dve.wait_ge(consts_landed, 16 * N_LOADS)
                dve.wait_ge(bias_prod, 1)
                TT(vec[:], ps[0:N_BIAS + 1, 7, 0:NJ], block_sb[:], ALU.add).then_inc(misc_read, 1)
                for l in range(DEPTH):
                    for k in range(2):
                        V.tensor_tensor_reduce(lam_junk[:], lamv[:, l, 2 * k, :], lamv[:, l, 2 * k + 1, :], 1.0, 0.0,
                                               ALU.mult, ALU.add, lam_s[:, l, k:k + 1]).then_inc(lam_sum, 1)
                        dve.wait_ge(lam_sum, 2 * l + k + 1)
                    step(TS(subg[:, l, :], subg[:, l, :], 1.0 - lam_init(l), None, ALU.mult))
                dve.wait_ge(consts_split_hi, 2)
                TT(wf_lo[:], wf[:], wf_hi[:].bitcast(F32), ALU.subtract).then_inc(consts_split_lo, 1)
                TT(wr_lo[:], wr[:], wr_hi[:].bitcast(F32), ALU.subtract).then_inc(consts_split_lo, 1)
                dve.wait_ge(lam_exp, 1)
                for l in range(DEPTH):
                    step(TT(neg_lam[:, l:l + 1], lam_s[:, l, 3:4], lam_s[:, l, 2:3], ALU.subtract))
                    step(TS(neg_lam[:, l:l + 1], neg_lam[:, l:l + 1], -lam_init(l), None, ALU.add))

            V.memset(mod[:, 0, :], 0.0).then_inc(part0_cleared, 1)
            dve.wait_ge(cs_ready, 1)
            first, ops = plan.segments["start"]
            units = first + [u for *_, ahead in ops for u in ahead]
            for u in units[:-4]:
                use(u)
            small_parameters()
            for u in units[-4:]:
                use(u)
            norm_factor(0)
            for kind, unit, a, ahead in ops:
                if kind == "mod_sum":
                    scale_part(a)
            dve.wait_ge(misc_read, plan.part_ready[0, 0])
            modulate(0, A1, SH1)
            turn_low(0)
            mixer(0)
            dve.wait_ge(misc_read, plan.part_ready[0, 2])
            modulate(1, A2, SH2)
            turn_low(2)
            dense()
            modulate(2, A1, SH1)
            turn_low(3)
            mixer(1)
            modulate(3, A2, SH2)
            turn_low(5)
            dve.wait_ge(hh_done, 1)
            dve.wait_ge(h_ready, 16)
            TT(hl[:], htok[:], hh[:].bitcast(F32), ALU.subtract).then_inc(hl_done, 1)
            experts(0)
            dve.wait_ge(flag_done, 1)
            more = dve.value_load(flag[0:1, 0:1], min_val=0, max_val=1)
            with dve.If(more > 0):
                experts(1)
            for i in range(NT):
                step(TT(moe[:, i, :], moe[:, i, :], G2, ALU.mult))
                TT(x[:, i, :], x[:, i, :], moe[:, i, :], ALU.add).then_inc(h_final, 1)
            dve.wait_ge(final_sq, 2)
            rstd(V, step, RS, SQ, 20, NT, D)
            dve.wait_ge(gain_landed, 16 * 5)
            for i in range(NT):
                STT(x[:, i, :], x[:, i, :], stat[:, RS + i:RS + i + 1], gain[:], ALU.mult, ALU.mult)\
                    .then_inc(out_ready, 1)


_INS = ["x", "c", "norm_mix_g", "norm_ffn_g", "w_mod", "b_mod", "w_in", "b_forget", "lam_q1", "lam_k1", "lam_q2",
        "lam_k2", "subln_g", "rel_bias", "w_br_a", "w_br_b", "w_br_c", "w_out", "w_ff_gate", "w_ff_up",
        "w_ff_down", "w_router", "w_exp_gate", "w_exp_up", "w_exp_down", "final_norm_g"]


def kernel(**inputs):
    import concourse.bacc as bacc
    from concourse.bass_utils import run_bass_kernel_spmd

    nc = bacc.Bacc("TRN2", target_bir_lowering=False, num_devices=1)
    arrays = {f"in_{name}": np.ascontiguousarray(inputs[name]) for name in _INS}
    arrays["in_buckets"], arrays["in_blocked"] = shape_tables()
    args = [nc.dram_tensor(name, a.shape, mybir.dt.from_np(a.dtype), kind="ExternalInput").ap()
            for name, a in arrays.items()]
    out = nc.dram_tensor("out_0", (1, S, D), F32, kind="ExternalOutput").ap()
    trunk(nc, *args, out)
    r = run_bass_kernel_spmd(nc, [arrays], core_ids=[0])
    return r.results[0]["out_0"]
```
